# Optimizing a Trainium2 kernel written in Bass

```python
import math
import jax, jax.numpy as jnp
from jax import lax
import numpy as np

D_MODEL = 1024
BATCH = 1
SEQ = 512
DEPTH = 2
DEC_BATCH = 1
DEC_SEQ = 512
PAST_LEN = 128

HEAD_DIM = 64
ROPE_THETA = 10000.0
NEG_INF = -1e30
RMS_EPS = 1e-6

MLA_HEADS = 8
MLA_Q_RANK = 384
MLA_KV_RANK = 256
MLA_NOPE = 64
MLA_ROPE = 32
MLA_V = 64
MLA_Q_BLOCK = 128

SWA_HEADS = 8
SWA_KV_HEADS = 2
SWA_GROUP = SWA_HEADS // SWA_KV_HEADS
SWA_HALF_WINDOW = 128
SWA_BLOCK = 128

DIL_HEADS = 8
DIL_BRANCHES = ((128, 1), (512, 4), (2048, 16))

NA_HEADS = 8
GRID_W = 64
NA_MAX_KH = 8
NA_KW = 16
NA_COL_BLOCK = 16

AB_IN = MLA_Q_RANK + MLA_KV_RANK + MLA_ROPE + (SWA_HEADS + 2 * SWA_KV_HEADS) * HEAD_DIM
AB_OUT = MLA_HEADS * MLA_V + SWA_HEADS * HEAD_DIM
CD_IN = 3 * (DIL_HEADS + NA_HEADS) * HEAD_DIM
CD_OUT = (DIL_HEADS + NA_HEADS) * HEAD_DIM

N_EXPERTS = 16
EC_CAPACITY_FACTOR = 2
D_EXPERT = 1024

N_EVEN = (DEPTH + 1) // 2
N_ODD = DEPTH // 2

kernel_name = 'hybrid_bidir_mla_swa_dilated_natten_ec_moe'

def rms_norm(x, g):
    xf = x.astype(jnp.float32)
    y = xf * lax.rsqrt(jnp.mean(xf * xf, axis=-1, keepdims=True) + RMS_EPS)
    return (y * g.astype(jnp.float32)).astype(x.dtype)

def rope_tables(n, dim):
    inv = 1.0 / (ROPE_THETA ** (jnp.arange(0, dim, 2, dtype=jnp.float32) / dim))
    ang = jnp.arange(n, dtype=jnp.float32)[:, None] * inv[None, :]
    return jnp.cos(ang), jnp.sin(ang)

def apply_rope(x, cos, sin):
    x1, x2 = jnp.split(x, 2, axis=-1)
    c = cos[None, :, None, :].astype(x.dtype)
    s = sin[None, :, None, :].astype(x.dtype)
    return jnp.concatenate([x1 * c - x2 * s, x1 * s + x2 * c], axis=-1)

def banded_attention(q, k, v, half_window, blk):
    n, L, G, R, dh = q.shape
    nb = -(-L // blk)
    pad = nb * blk - L
    qb = jnp.pad(q, ((0, 0), (0, pad), (0, 0), (0, 0), (0, 0))).reshape(n, nb, blk, G, R, dh)

    def windows(t):
        tp = jnp.pad(t, ((0, 0), (blk, pad + blk), (0, 0), (0, 0))).reshape(n, nb + 2, blk, G, dh)
        return jnp.concatenate([tp[:, :-2], tp[:, 1:-1], tp[:, 2:]], axis=2)

    kw, vw = windows(k), windows(v)
    qpos = jnp.arange(nb * blk).reshape(nb, blk)
    kpos = jnp.arange(-blk, (nb + 1) * blk).reshape(nb + 2, blk)
    kpos = jnp.concatenate([kpos[:-2], kpos[1:-1], kpos[2:]], axis=1)
    valid = ((jnp.abs(qpos[:, :, None] - kpos[:, None, :]) <= half_window)
             & (kpos[:, None, :] >= 0) & (kpos[:, None, :] < L))
    s = jnp.einsum('nbqgrd,nbkgd->nbgrqk', qb, kw).astype(jnp.float32) * (dh ** -0.5)
    s = jnp.where(valid[None, :, None, None], s, NEG_INF)
    m = jnp.max(s, axis=-1, keepdims=True)
    p = jnp.exp(s - m)
    den = jnp.sum(p, axis=-1, keepdims=True)
    o = jnp.einsum('nbgrqk,nbkgd->nbqgrd', (p / den).astype(v.dtype), vw)
    lse = jnp.transpose((m + jnp.log(den))[..., 0], (0, 1, 4, 2, 3))
    o = o.reshape(n, nb * blk, G, R, dh)[:, :L]
    lse = lse.reshape(n, nb * blk, G, R)[:, :L]
    return o, lse

def mla_attention(q_nope, q_rope, k_nope, k_rope, v):
    B, S, H, _ = q_nope.shape
    nb = S // MLA_Q_BLOCK
    scale = (MLA_NOPE + MLA_ROPE) ** -0.5
    qn = q_nope.reshape(B, nb, MLA_Q_BLOCK, H, MLA_NOPE).transpose(1, 0, 2, 3, 4)
    qr = q_rope.reshape(B, nb, MLA_Q_BLOCK, H, MLA_ROPE).transpose(1, 0, 2, 3, 4)

    def block(args):
        qn_b, qr_b = args
        s = (jnp.einsum('bqhd,bkhd->bhqk', qn_b, k_nope)
             + jnp.einsum('bqhd,bkd->bhqk', qr_b, k_rope)).astype(jnp.float32) * scale
        p = jax.nn.softmax(s, axis=-1)
        return jnp.einsum('bhqk,bkhd->bqhd', p.astype(v.dtype), v)

    out = lax.map(block, (qn, qr))
    return out.transpose(1, 0, 2, 3, 4).reshape(B, S, H, MLA_V)

def dilated_attention(q, k, v):
    B, S, H, dh = q.shape
    outs, lses = [], []
    for window, dil in DIL_BRANCHES:
        L = S // dil
        half = window // (2 * dil)

        def to_stream(t):
            return t.reshape(B, L, dil, H, dh).transpose(0, 2, 1, 3, 4).reshape(B * dil, L, H, dh)

        o, lse = banded_attention(to_stream(q)[:, :, :, None, :], to_stream(k), to_stream(v), half, half)
        outs.append(o[:, :, :, 0].reshape(B, dil, L, H, dh).transpose(0, 2, 1, 3, 4).reshape(B, S, H, dh))
        lses.append(lse[..., 0].reshape(B, dil, L, H).transpose(0, 2, 1, 3).reshape(B, S, H))
    w = jax.nn.softmax(jnp.stack(lses), axis=0)
    return jnp.einsum('nbsh,nbshd->bshd', w.astype(q.dtype), jnp.stack(outs))

def neighborhood_attention(q, k, v, rpb):
    B, S, H, dh = q.shape
    rows = S // GRID_W
    kh = min(NA_MAX_KH, rows)
    scale = dh ** -0.5
    qg = q.reshape(B, rows, GRID_W, H, dh).transpose(1, 0, 2, 3, 4)
    kg = k.reshape(B, rows, GRID_W, H, dh)
    vg = v.reshape(B, rows, GRID_W, H, dh)
    ncb = GRID_W // NA_COL_BLOCK
    span = NA_COL_BLOCK + NA_KW
    col_q = jnp.arange(GRID_W).reshape(ncb, NA_COL_BLOCK)
    kb_start = jnp.clip(jnp.arange(ncb) * NA_COL_BLOCK - NA_KW // 2, 0, GRID_W - span)
    col_k = kb_start[:, None] + jnp.arange(span)[None, :]
    win_c0 = jnp.clip(col_q - NA_KW // 2, 0, GRID_W - NA_KW)
    col_valid = ((col_k[:, None, :] >= win_c0[..., None])
                 & (col_k[:, None, :] < win_c0[..., None] + NA_KW))
    col_idx = jnp.clip(col_k[:, None, :] - col_q[..., None] + NA_KW - 1, 0, 2 * NA_KW - 2)
    row_start = jnp.clip(jnp.arange(rows) - kh // 2, 0, rows - kh)

    def row_block(args):
        r, r0, q_row = args
        k_rows = lax.dynamic_slice_in_dim(kg, r0, kh, axis=1)
        v_rows = lax.dynamic_slice_in_dim(vg, r0, kh, axis=1)
        k_cb = k_rows[:, :, col_k]
        v_cb = v_rows[:, :, col_k]
        q_cb = q_row.reshape(B, ncb, NA_COL_BLOCK, H, dh)
        s = jnp.einsum('bcqhd,bjcshd->bhcqjs', q_cb, k_cb).astype(jnp.float32) * scale
        row_idx = r0 + jnp.arange(kh) - r + NA_MAX_KH - 1
        bias = rpb[:, row_idx[None, None, :, None], col_idx[:, :, None, :]]
        s = s + bias[None].astype(jnp.float32)
        s = jnp.where(col_valid[None, None, :, :, None, :], s, NEG_INF)
        p = jax.nn.softmax(s, axis=(-2, -1))
        o = jnp.einsum('bhcqjs,bjcshd->bcqhd', p.astype(v.dtype), v_cb)
        return o.reshape(B, GRID_W, H, dh)

    out = lax.map(row_block, (jnp.arange(rows), row_start, qg))
    return out.transpose(1, 0, 2, 3, 4).reshape(B, S, H, dh)

def mixer_mla_swa(h, w_in, q_norm, w_uq, kv_norm, w_ukv, sink, w_out):
    B, S, _ = h.shape
    proj = h @ w_in
    cuts = np.cumsum([MLA_Q_RANK, MLA_KV_RANK, MLA_ROPE, SWA_HEADS * HEAD_DIM, SWA_KV_HEADS * HEAD_DIM])
    c_q, c_kv, k_r, q_b, k_b, v_b = jnp.split(proj, [int(c) for c in cuts], axis=-1)
    q = (rms_norm(c_q, q_norm) @ w_uq).reshape(B, S, MLA_HEADS, MLA_NOPE + MLA_ROPE)
    kv = (rms_norm(c_kv, kv_norm) @ w_ukv).reshape(B, S, MLA_HEADS, MLA_NOPE + MLA_V)
    cos_r, sin_r = rope_tables(S, MLA_ROPE)
    q_rope = apply_rope(q[..., MLA_NOPE:], cos_r, sin_r)
    k_rope = apply_rope(k_r[:, :, None, :], cos_r, sin_r)[:, :, 0]
    o_a = mla_attention(q[..., :MLA_NOPE], q_rope, kv[..., :MLA_NOPE], k_rope, kv[..., MLA_NOPE:])
    cos, sin = rope_tables(S, HEAD_DIM)
    qb = apply_rope(q_b.reshape(B, S, SWA_HEADS, HEAD_DIM), cos, sin).reshape(B, S, SWA_KV_HEADS, SWA_GROUP, HEAD_DIM)
    kb = apply_rope(k_b.reshape(B, S, SWA_KV_HEADS, HEAD_DIM), cos, sin)
    vb = v_b.reshape(B, S, SWA_KV_HEADS, HEAD_DIM)
    o_b, lse = banded_attention(qb, kb, vb, SWA_HALF_WINDOW, SWA_BLOCK)
    keep = jax.nn.sigmoid(lse - sink.reshape(SWA_KV_HEADS, SWA_GROUP).astype(jnp.float32))
    o_b = o_b * keep[..., None].astype(o_b.dtype)
    o = jnp.concatenate([o_a.reshape(B, S, MLA_HEADS * MLA_V), o_b.reshape(B, S, SWA_HEADS * HEAD_DIM)], axis=-1)
    return o @ w_out

def mixer_dilated_natten(h, w_in, rpb, w_out):
    B, S, _ = h.shape
    proj = h @ w_in
    q_c, k_c, v_c, q_d, k_d, v_d = jnp.split(proj, 6, axis=-1)
    cos, sin = rope_tables(S, HEAD_DIM)
    shp = (B, S, DIL_HEADS, HEAD_DIM)
    o_c = dilated_attention(apply_rope(q_c.reshape(shp), cos, sin), apply_rope(k_c.reshape(shp), cos, sin), v_c.reshape(shp))
    shp_d = (B, S, NA_HEADS, HEAD_DIM)
    o_d = neighborhood_attention(q_d.reshape(shp_d), k_d.reshape(shp_d), v_d.reshape(shp_d), rpb)
    o = jnp.concatenate([o_c.reshape(B, S, DIL_HEADS * HEAD_DIM), o_d.reshape(B, S, NA_HEADS * HEAD_DIM)], axis=-1)
    return o @ w_out

def expert_choice_ffn(h, w_router, w_gate, w_up, w_down):
    shp = h.shape
    xt = h.reshape(-1, shp[-1])
    T = xt.shape[0]
    cap = EC_CAPACITY_FACTOR * T // N_EXPERTS
    aff = jax.nn.softmax((xt @ w_router).astype(jnp.float32), axis=-1)
    gate, idx = lax.top_k(aff.T, cap)
    xe = xt[idx]
    g = jnp.einsum('ecd,edf->ecf', xe, w_gate)
    u = jnp.einsum('ecd,edf->ecf', xe, w_up)
    ye = jnp.einsum('ecf,efd->ecd', jax.nn.silu(g) * u, w_down) * gate[..., None].astype(xt.dtype)
    y = jnp.zeros_like(xt).at[idx.reshape(-1)].add(ye.reshape(-1, shp[-1]))
    return y.reshape(shp)

def trunk(x, norm_mix, norm_ffn, norm_final, w_in_ab, mla_q_norm, mla_w_uq, mla_kv_norm, mla_w_ukv,
          swa_sink, w_out_ab, w_in_cd, na_rpb, w_out_cd, w_router, w_gate, w_up, w_down):
    for l in range(DEPTH):
        i = l // 2
        h = rms_norm(x, norm_mix[l])
        if l % 2 == 0:
            x = x + mixer_mla_swa(h, w_in_ab[i], mla_q_norm[i], mla_w_uq[i], mla_kv_norm[i], mla_w_ukv[i],
                                  swa_sink[i], w_out_ab[i])
        else:
            x = x + mixer_dilated_natten(h, w_in_cd[i], na_rpb[i], w_out_cd[i])
        h = rms_norm(x, norm_ffn[l])
        x = x + expert_choice_ffn(h, w_router[l], w_gate[l], w_up[l], w_down[l])
    return rms_norm(x, norm_final)

def setup_inputs(seed: int = 0) -> dict:
    key = jax.random.key(seed)
    ks = jax.random.split(key, 20)

    def nrm(k, shape, scale):
        return jax.random.normal(k, shape, jnp.float32) * scale

    return {
        'x_prompt': nrm(ks[0], (BATCH, SEQ, D_MODEL), 1.0),
        'x_sample': nrm(ks[1], (DEC_BATCH, DEC_SEQ, D_MODEL), 1.0),
        'norm_mix': 1.0 + nrm(ks[2], (DEPTH, D_MODEL), 0.02),
        'norm_ffn': 1.0 + nrm(ks[3], (DEPTH, D_MODEL), 0.02),
        'norm_final': 1.0 + nrm(ks[4], (D_MODEL,), 0.02),
        'w_in_ab': nrm(ks[5], (N_EVEN, D_MODEL, AB_IN), D_MODEL ** -0.5),
        'mla_q_norm': 1.0 + nrm(ks[6], (N_EVEN, MLA_Q_RANK), 0.02),
        'mla_w_uq': nrm(ks[7], (N_EVEN, MLA_Q_RANK, MLA_HEADS * (MLA_NOPE + MLA_ROPE)), MLA_Q_RANK ** -0.5),
        'mla_kv_norm': 1.0 + nrm(ks[8], (N_EVEN, MLA_KV_RANK), 0.02),
        'mla_w_ukv': nrm(ks[9], (N_EVEN, MLA_KV_RANK, MLA_HEADS * (MLA_NOPE + MLA_V)), MLA_KV_RANK ** -0.5),
        'swa_sink': nrm(ks[10], (N_EVEN, SWA_HEADS), 1.0),
        'w_out_ab': nrm(ks[11], (N_EVEN, AB_OUT, D_MODEL), AB_OUT ** -0.5),
        'w_in_cd': nrm(ks[12], (N_ODD, D_MODEL, CD_IN), D_MODEL ** -0.5),
        'na_rpb': nrm(ks[13], (N_ODD, NA_HEADS, 2 * NA_MAX_KH - 1, 2 * NA_KW - 1), 0.1),
        'w_out_cd': nrm(ks[14], (N_ODD, CD_OUT, D_MODEL), CD_OUT ** -0.5),
        'w_router': nrm(ks[15], (DEPTH, D_MODEL, N_EXPERTS), D_MODEL ** -0.5),
        'w_gate': nrm(ks[16], (DEPTH, N_EXPERTS, D_MODEL, D_EXPERT), D_MODEL ** -0.5),
        'w_up': nrm(ks[17], (DEPTH, N_EXPERTS, D_MODEL, D_EXPERT), D_MODEL ** -0.5),
        'w_down': nrm(ks[18], (DEPTH, N_EXPERTS, D_EXPERT, D_MODEL), D_EXPERT ** -0.5),
    }

def reference(x_prompt, x_sample, norm_mix, norm_ffn, norm_final, w_in_ab, mla_q_norm, mla_w_uq, mla_kv_norm,
              mla_w_ukv, swa_sink, w_out_ab, w_in_cd, na_rpb, w_out_cd, w_router, w_gate, w_up, w_down):
    y_prompt = trunk(x_prompt, norm_mix, norm_ffn, norm_final, w_in_ab, mla_q_norm, mla_w_uq, mla_kv_norm,
                     mla_w_ukv, swa_sink, w_out_ab, w_in_cd, na_rpb, w_out_cd, w_router, w_gate, w_up, w_down)
    y_sample = trunk(x_sample, norm_mix, norm_ffn, norm_final, w_in_ab, mla_q_norm, mla_w_uq, mla_kv_norm,
                     mla_w_ukv, swa_sink, w_out_ab, w_in_cd, na_rpb, w_out_cd, w_router, w_gate, w_up, w_down)
    return (y_prompt, y_sample)


_drawn_inputs = setup_inputs


def setup_inputs(seed=0):
    import zlib

    import numpy as np

    out = dict(_drawn_inputs(seed))
    spreads = {}
    factors = {'norm_mix': 4.468,
     'norm_final': 8.255,
     'mla_q_norm': 6.854,
     'mla_kv_norm': 5.755,
     'swa_sink': 8.0,
     'na_rpb': 3.61,
     'norm_ffn': 3.977}
    for name, (base, spread) in spreads.items():
        noise = np.random.default_rng([zlib.crc32(name.encode()), seed]).standard_normal(out[name].shape)
        drawn = base * np.exp(spread * noise) if base else spread * noise
        out[name] = __import__('jax').numpy.asarray(drawn.astype(out[name].dtype))
    for name, factor in factors.items():
        out[name] = (out[name] * factor).astype(out[name].dtype)
    return out
```

```python
from contextlib import ExitStack

import concourse.bass as bass
from concourse import mybir

F32 = mybir.dt.float32
U32 = mybir.dt.uint32
ALU = mybir.AluOpType
ACT = mybir.ActivationFunctionType
AX = mybir.AxisListType

P = 128
D = 1024
SEQ = 512
SEQS = 2
T = SEQ // P
TOK = SEQS * SEQ
DC = D // P
BANK = 512
EPS = 1e-6
NEG = -1e30
BIG = 3e38

QR, KVR, ROPE, NOPE, MV = 384, 256, 32, 64, 64
H = 8
HD = 64
KVH = 2
G = H // KVH
MQ = NOPE + ROPE
AB_IN = QR + KVR + ROPE + (H + 2 * KVH) * HD
CD_IN = 6 * H * HD
SPAN = 2 * SEQ - P
E = 16
CAP = 64
F = 1024
GRID_W = 64
CREDIT = 256


class Steps:

    def __init__(self, counts, engine, names, rounds, lead=0):
        self.sem, start = counts[engine]
        self.base = start + lead
        self.index = {name: k for k, name in enumerate(names)}
        self.per = len(names)
        assert len(self.index) == self.per
        counts[engine] = (self.sem, self.base + self.per * rounds)
        self.told = []

    def after(self, name, n=0):
        return n * self.per + (self.base + self.index[name] + 1)

    def done(self, name, instruction):
        assert self.index[name] == len(self.told) % self.per, name
        self.told.append(name)
        instruction.then_inc(self.sem, 1)


def hybrid_trunk(nc, x_in, norm_mix, norm_ffn, norm_final, w_in_ab, q_norm, w_uq, kv_norm, w_ukv, sink,
                 w_out_ab, w_in_cd, rpb_padded, w_out_cd, w_router, w_gate, w_up, w_down,
                 rope_table, window_table, dilated_table, column_table, y_out):
    with ExitStack() as ctx:
        def sb(name, shape, dt=F32):
            return ctx.enter_context(nc.sbuf_tensor(name, shape, dt))

        def sem(name):
            return ctx.enter_context(nc.semaphore(name))

        def dram(name, shape):
            return nc.dram_tensor(name, shape, F32, kind="Internal").ap()

        def at(a, offset, pattern):
            return bass.AP(a.tensor, offset, pattern)

        WIDTHS = (D, QR, KVR)
        RING = 6
        PIECE = 4 * 1024
        ring = sb("ring", [P, RING * PIECE])
        ARENA = 27136
        arena = sb("arena", [P, ARENA])
        ident = sb("ident", [P, P])
        minus_half = sb("minus_half", [P, 1])
        epsilon = sb("epsilon", [P, 1])
        one_over = sb("one_over", [P, 3])
        rows_to_slots = sb("rows_to_slots", [48, E])
        aff_turned = sb("aff_turned", [48, SEQ])
        chosen = sb("chosen", [P, E + 1], U32)
        gates = sb("gates", [P, E + 1])
        bank = [ctx.enter_context(nc.psum_tensor(f"bank{b}", [P, BANK], F32)) for b in range(8)]

        class Arena:
            def __init__(self):
                self.at = 0

            def take(self, *shape, rows=P):
                n = 1
                for k in shape:
                    n *= k
                v = arena[0:rows, self.at:self.at + n]
                self.at += n
                assert self.at <= ARENA, self.at
                if len(shape) == 1:
                    return v
                letters = "abcd"[:len(shape)]
                sizes = dict(zip(letters, shape))
                return v.rearrange(f"p ({' '.join(letters)}) -> p {' '.join(letters)}", **sizes)

        residual = dram("residual", [TOK, D])
        normed = dram("normed", [TOK, D])
        mixed = dram("mixed", [TOK, D])
        grid_bias = dram("grid_bias", [H, P, SPAN])
        qkv = {kind: (dram(f"q_{kind}", [8, w, n * P]), dram(f"k_{kind}", [8, w, n * P]),
                      dram(f"v_{kind}", [8, P, H * HD]))
               for kind, w, n in (("mla", MQ, H), ("window", P, H // 2), ("dilated", P, H // 2), ("grid", P, H // 2))}

        PAIR_TILE = P * (H // 2) * P

        counts = {e: (sem(f"{e}_steps"), CREDIT) for e in ("pe", "act", "dve", "pool")}
        stage_ended = sem("stage_ended")
        waited = {e.engine: sem(f"{name}_waited")
                  for name, e in (("dve", nc.vector), ("pe", nc.tensor), ("pool", nc.gpsimd), ("sp", nc.sync))}
        ident_ready = sem("ident_ready")
        piece_in = [sem(f"piece_in{k}") for k in range(RING)]
        pieces = [0] * RING

        block_programs = {"sp": [], "pe": [], "act": [], "dve": [], "pool": []}

        def barrier(index):
            def wait_for_all(eng):
                eng.drain().then_inc(stage_ended, 1)
                eng.wait_ge(stage_ended, 5 * index)
            return wait_for_all

        n_barriers = [0]

        def end_stage(sp, pe, act, dve, pool):
            n_barriers[0] += 1
            wait_for_all = barrier(n_barriers[0])
            for name, program in (("sp", sp), ("pe", pe), ("act", act), ("dve", dve), ("pool", pool)):
                block_programs[name] += [program, wait_for_all]

        def start():
            setup = sem("setup")

            def sp(eng):
                pass

            def pe(eng):
                eng.sem_inc(counts["pe"][0], CREDIT)

            def act(eng):
                eng.sem_inc(counts["act"][0], CREDIT)

            def dve(eng):
                eng.sem_inc(counts["dve"][0], CREDIT)
                eng.wait_ge(setup, 9)
                eng.tensor_copy(rows_to_slots[0:16, :], ident[0:16, 0:16])
                eng.tensor_copy(rows_to_slots[32:48, :], ident[32:48, 32:48])

            def pool(eng):
                eng.sem_inc(counts["pool"][0], CREDIT)
                eng.memset(ident[:, :], 0.0).then_inc(setup, 1)
                eng.memset(minus_half[:, :], -0.5).then_inc(setup, 1)
                eng.memset(rows_to_slots[:, :], 0.0).then_inc(setup, 1)
                eng.memset(gates[:, :], 0.0).then_inc(setup, 1)
                eng.memset(epsilon[:, :], EPS).then_inc(setup, 1)
                for k, width in enumerate(WIDTHS):
                    eng.memset(one_over[:, k:k + 1], 1.0 / width).then_inc(setup, 1)
                eng.wait_ge(setup, 8)
                eng.affine_select(out=ident[:, :], in_=ident[:, :], compare_op=ALU.not_equal, fill=1.0,
                                  base=0, pattern=[[-1, P]], channel_multiplier=1).then_inc(setup, 1)

            end_stage(sp, pe, act, dve, pool)

        def passed(eng):
            eng.sem_inc(waited[eng.engine], 1)

        def rsqrt_mean(eng, steps, name, n, total, mean, out, width):
            inverse = one_over[:, WIDTHS.index(width):WIDTHS.index(width) + 1]
            steps.done(name + " mean", eng.tensor_tensor(mean, total, inverse, ALU.mult))
            eng.wait_ge(steps.sem, steps.after(name + " mean", n))
            steps.done(name + " eps", eng.tensor_tensor(mean, mean, epsilon[:, :], ALU.add))
            eng.wait_ge(steps.sem, steps.after(name + " eps", n))
            steps.done(name, eng.tensor_tensor(out, mean, minus_half[:, :], ALU.pow))

        def project(kind, layer, source):
            ab = kind == "ab"
            a = Arena()
            gain = a.take(D)
            qgain, kvgain = (a.take(QR), a.take(KVR)) if ab else (None, None)
            xt = [a.take(D) for _ in range(2)]
            ht = [a.take(D) for _ in range(2)]
            hT = [a.take(DC, P) for _ in range(2)]
            rt = [a.take(6, 64) for _ in range(2)]
            st = [a.take(16) for _ in range(2)]
            win_cols = AB_IN if ab else CD_IN
            w_in = ring[:, 0:DC * win_cols].rearrange("p (c n) -> p c n", c=DC)
            w_dram = w_in_ab if ab else w_in_cd
            if ab:
                o = DC * AB_IN
                wuq = ring[:, o:o + 3 * H * MQ].rearrange("p (c n) -> p c n", c=3)
                o += 3 * H * MQ
                wukv = ring[:, o:o + 2 * H * 128].rearrange("p (c n) -> p c n", c=2)
                assert o + 2 * H * 128 <= 4 * PIECE
                qrow = [a.take(H, MQ) for _ in range(2)]
                krow = [a.take(H, MQ) for _ in range(2)]
                vrow = [a.take(H, MV) for _ in range(2)]
                kr = [a.take(2, ROPE) for _ in range(2)]
                mtmp = [a.take(H + 1, ROPE) for _ in range(2)]
                cqn = [a.take(3, P) for _ in range(2)]
                ckvn = [a.take(2, P) for _ in range(2)]
                cqT = [a.take(3, P) for _ in range(2)]
                ckvT = [a.take(2, P) for _ in range(2)]
                mqT = [a.take(H, P, rows=MQ) for _ in range(2)]
                mkT = [a.take(H, P, rows=MQ) for _ in range(2)]
                squares_out = [a.take(QR + KVR) for _ in range(2)]
                sq = [a.take(H, 64) for _ in range(2)]
                sq2 = [a.take(H, 64) for _ in range(2)]
                sk = [a.take(KVH, 64) for _ in range(2)]
                sk2 = [a.take(KVH, 64) for _ in range(2)]
                sv = [a.take(H, 64) for _ in range(2)]
                sqT = [a.take(4, P) for _ in range(2)]
                skT = [a.take(P) for _ in range(2)]
            else:
                rows = {m: [a.take(H, 64) for _ in range(2)] for m in ("qc", "kc", "vc", "qd", "kd", "vd")}
                rows2 = {m: [a.take(H, 64) for _ in range(2)] for m in ("qc", "kc")}
                turned = {m: [a.take(4, P) for _ in range(2)] for m in ("qc", "kc", "qd", "kd")}

            weights_in = sem(f"{kind}_weights_in")
            bias_spread = sem("bias_spread") if ab else None
            gain_in = sem(f"{kind}_gain_in")
            x_in_s = [sem(f"{kind}_x_in{s}") for s in range(2)]
            rows_out = [sem(f"{kind}_rows_out{s}") for s in range(2)]
            ROUNDS = SEQS * T

            if ab:
                pe_names = ["h0", "h1", "cq", "ckv", "qb", "kvb", "cq turn", "ckv turn", "q0", "q1", "kv0", "kv1",
                            "sq turn", "q turn0", "q turn1", "k turn0", "k turn1"]
                bank_of = dict(zip(pe_names, [0, 1, 2, 3, 4, 5, 6, 7, 2, 3, 4, 5, 6, 0, 1, 2, 3]))
                act_names = ["square", "h0", "cq square", "ckv square", "cq turn", "q0", "q1", "sq turn",
                             "q turn0", "q turn1"]
                dve_names = ["h", "h1", "cqn", "ckvn", "kr", "qb", "sv", "kvb", "ckv turn", "sk turn", "kv0", "kv1",
                             "k turn0", "k turn1"]
                pool_names = ["x mean", "x eps", "x", "cq mean", "cq eps", "cq", "ckv mean", "ckv eps", "ckv",
                              "kr a", "kr b", "kr sum", "sq", "sk",
                              "q rope a", "q rope b", "q rope sum"]
                emptied = {"h0": "act", "h1": "dve", "cq": ("dve", "cqn"), "ckv": ("dve", "kr"), "qb": "dve",
                           "kvb": "dve", "cq turn": "act", "ckv turn": ("dve", "sk turn"), "q0": "act", "q1": "act",
                           "kv0": "dve", "kv1": "dve", "sq turn": "act", "q turn0": "act", "q turn1": "act",
                           "k turn0": "dve", "k turn1": "dve"}
            else:
                prods = ["qc", "kc", "vc", "qd", "kd", "vd"]
                turns = ["qc", "kc", "qd", "kd"]
                pe_names = ["h0", "h1"] + prods + [m + " turn" for m in turns]
                bank_of = dict(zip(pe_names, [0, 1, 2, 3, 4, 5, 6, 7, 2, 3, 5, 6]))
                act_names = ["square", "h0", "vc", "qd", "vd", "qc turn", "qd turn"]
                dve_names = ["h", "h1", "qc", "kc", "kd", "kc turn", "kd turn"]
                pool_names = ["x mean", "x eps", "x", "qc", "kc"]
                emptied = {"h0": "act", "h1": "dve", "qc": "dve", "kc": "dve", "vc": "act", "qd": "act", "kd": "dve",
                           "vd": "act", "qc turn": "act", "qd turn": "act", "kc turn": "dve", "kd turn": "dve"}
            pe_s = Steps(counts, "pe", pe_names, ROUNDS)
            act_s = Steps(counts, "act", act_names, ROUNDS)
            dve_s = Steps(counts, "dve", dve_names, ROUNDS)
            pool_s = Steps(counts, "pool", pool_names, ROUNDS)
            by = {"act": act_s, "dve": dve_s}

            def wait_bank_empty(eng, name, n):
                b = bank_of[name]
                users = [m for m in pe_names if bank_of[m] == b]
                k = users.index(name)
                last, m = (users[k - 1], n) if k else (users[-1], n - 1)
                who = emptied[last]
                who, step = who if isinstance(who, tuple) else (who, last)
                eng.wait_ge(by[who].sem, by[who].after(step, m))

            def sp(eng):
                eng.dma_start(gain, at(norm_mix, layer * D, [[0, P], [1, D]])).then_inc(gain_in, 16)
                if ab:
                    eng.dma_start(qgain, at(q_norm, 0, [[0, P], [1, QR]])).then_inc(gain_in, 16)
                    eng.dma_start(kvgain, at(kv_norm, 0, [[0, P], [1, KVR]])).then_inc(gain_in, 16)

                def load(t, s):
                    eng.dma_start(xt[s], at(source, (t + T * s) * P * D, [[D, P], [1, D]])).then_inc(x_in_s[s], 16)
                    eng.dma_start(rt[s].rearrange("p a b -> p (a b)"),
                                  at(rope_table, t * P * 384, [[384, P], [1, 384]])).then_inc(x_in_s[s], 16)

                load(0, 0)
                for c in range(DC):
                    eng.dma_start(w_in[:, c, :], w_dram[c * P:(c + 1) * P, :]).then_inc(weights_in, 16)
                if ab:
                    eng.dma_start(wuq, w_uq.rearrange("(c p) n -> p c n", p=P)).then_inc(weights_in, 16)
                    eng.dma_start(wukv, w_ukv.rearrange("(c p) n -> p c n", p=P)).then_inc(weights_in, 16)
                load(0, 1)
                if ab:
                    for h in range(H):
                        for r in range(2):
                            eng.dma_start(at(grid_bias, (h * P + 64 * r) * SPAN, [[GRID_W, 14], [SPAN, 64], [1, GRID_W]]),
                                          at(rpb_padded, h * 15 * P + (1 - r) * P + 63, [[P, 14], [-1, 64], [1, GRID_W]])
                                          ).then_inc(bias_spread, 16)

                def store(t, s, n):
                    i = t + T * s
                    out = rows_out[s]
                    if ab:
                        qd, kd, vd = qkv["mla"]
                        w = MQ * H * P
                        eng.wait_ge(dve_s.sem, dve_s.after("kv1", n))
                        eng.dma_start(at(vd, i * P * H * HD, [[H * HD, P], [1, H * HD]]),
                                      vrow[s].rearrange("p a b -> p (a b)")).then_inc(out, 16)
                        qs, ks, vs = qkv["window"]
                        eng.dma_start(at(vs, i * P * H * HD, [[H * HD, P], [1, H * HD]]),
                                      sv[s].rearrange("p a b -> p (a b)")).then_inc(out, 16)
                        for g in range(KVH):
                            src = skT[s][64 * g:64 * g + 64, :]
                            src = src.rearrange("p (a n) -> p a n", a=1).to_broadcast([64, G // 2, P])
                            for e in range(2):
                                eng.dma_start(at(ks, i * PAIR_TILE + e * HD * 4 * P + g * (G // 2) * P,
                                                 [[4 * P, HD], [P, G // 2], [1, P]]), src).then_inc(out, 16)
                        eng.wait_ge(act_s.sem, act_s.after("sq turn", n))
                        eng.dma_start(at(qs, i * PAIR_TILE, [[4 * P, P], [1, 4 * P]]),
                                      sqT[s].rearrange("p a b -> p (a b)")).then_inc(out, 16)
                        eng.wait_ge(act_s.sem, act_s.after("q turn1", n))
                        eng.dma_start(at(qd, i * w, [[H * P, MQ], [1, H * P]]),
                                      mqT[s].rearrange("p a b -> p (a b)")).then_inc(out, 16)
                        eng.wait_ge(dve_s.sem, dve_s.after("k turn1", n))
                        eng.dma_start(at(kd, i * w, [[H * P, MQ], [1, H * P]]),
                                      mkT[s].rearrange("p a b -> p (a b)")).then_inc(out, 16)
                    else:
                        eng.wait_ge(act_s.sem, act_s.after("vd", n))
                        passed(eng)
                        for name, v in (("dilated", "vc"), ("grid", "vd")):
                            eng.dma_start(at(qkv[name][2], i * P * H * HD, [[H * HD, P], [1, H * HD]]),
                                          rows[v][s].rearrange("p a b -> p (a b)")).then_inc(out, 16)
                        eng.wait_ge(act_s.sem, act_s.after("qd turn", n))
                        passed(eng)
                        eng.wait_ge(dve_s.sem, dve_s.after("kd turn", n))
                        passed(eng)
                        for name, which, m in (("dilated", 0, "qc"), ("dilated", 1, "kc"),
                                               ("grid", 0, "qd"), ("grid", 1, "kd")):
                            eng.dma_start(at(qkv[name][which], i * PAIR_TILE, [[4 * P, P], [1, 4 * P]]),
                                          turned[m][s].rearrange("p a b -> p (a b)")).then_inc(out, 16)

                last = ("dve", "kvb") if ab else ("dve", "kc")
                with eng.Fori(0, T - 1) as t:
                    for s in range(2):
                        n = t * 2 + s
                        store(t, s, n)
                        if ab:
                            eng.wait_ge(pool_s.sem, pool_s.after("q rope sum", n))
                        load(t + 1, s)
                for s in range(2):
                    store(T - 1, s, 2 * (T - 1) + s)
                for s in range(2):
                    eng.wait_ge(rows_out[s], 16 * (NSTORE * T + 1))
                if ab:
                    eng.wait_ge(bias_spread, 16 * 2 * H)

            NSTORE = 9 if ab else 6

            def pe(eng):
                def product(name, n, shape_cols, lhs, rhs_of, chunks):
                    wait_bank_empty(eng, name, n)
                    for c in range(chunks):
                        mm = eng.matmul(bank[bank_of[name]][:, 0:shape_cols], lhs(c), rhs_of(c),
                                        start=(c == 0), stop=(c == chunks - 1))
                    pe_s.done(name, mm)

                with eng.Fori(0, T) as t:
                    for s in range(2):
                        n = t * 2 + s
                        eng.wait_ge(dve_s.sem, dve_s.after("h", n))
                        for k in range(2):
                            wait_bank_empty(eng, f"h{k}", n)
                            for c in range(4):
                                mm = eng.transpose(bank[k][:, c * P:(c + 1) * P],
                                                   ht[s][:, (4 * k + c) * P:(4 * k + c + 1) * P], ident[:, :])
                            pe_s.done(f"h{k}", mm)
                        eng.wait_ge(act_s.sem, act_s.after("h0", n))
                        eng.wait_ge(dve_s.sem, dve_s.after("h1", n))
                        eng.wait_ge(weights_in, 16 * (DC + 2 * ab))
                        lhs = lambda c: hT[s][:, c, :]
                        if ab:
                            cols = [("cq", 0, QR), ("ckv", QR, KVR + ROPE), ("qb", QR + KVR + ROPE, H * HD),
                                    ("kvb", QR + KVR + ROPE + H * HD, 2 * KVH * HD)]
                        else:
                            cols = [(m, k * H * HD, H * HD) for k, m in enumerate(prods)]
                        for name, first, width in cols:
                            product(name, n, width, lhs, lambda c: w_in[:, c, first:first + width], DC)
                        if ab:
                            eng.wait_ge(dve_s.sem, dve_s.after("cqn", n))
                            wait_bank_empty(eng, "cq turn", n)
                            for c in range(3):
                                mm = eng.transpose(bank[6][:, c * P:(c + 1) * P], cqn[s][:, c, :], ident[:, :])
                            pe_s.done("cq turn", mm)
                            eng.wait_ge(pool_s.sem, pool_s.after("sk", n))
                            eng.wait_ge(dve_s.sem, dve_s.after("ckvn", n))
                            wait_bank_empty(eng, "ckv turn", n)
                            for c in range(2):
                                eng.transpose(bank[7][:, c * P:(c + 1) * P], ckvn[s][:, c, :], ident[:, :])
                            pe_s.done("ckv turn", eng.transpose(
                                bank[7][:, 2 * P:3 * P], sk[s].rearrange("p a b -> p (a b)"), ident[:, :]))
                            eng.wait_ge(act_s.sem, act_s.after("cq turn", n))
                            for k in range(2):
                                product(f"q{k}", n, 4 * MQ, lambda c: cqT[s][:, c, :],
                                        lambda c: wuq[:, c, k * 4 * MQ:(k + 1) * 4 * MQ], 3)
                            eng.wait_ge(dve_s.sem, dve_s.after("ckv turn", n))
                            for k in range(2):
                                product(f"kv{k}", n, 512, lambda c: ckvT[s][:, c, :],
                                        lambda c: wukv[:, c, k * 512:(k + 1) * 512], 2)
                            wait_bank_empty(eng, "sq turn", n)
                            for c in range(4):
                                mm = eng.transpose(bank[6][:, c * P:(c + 1) * P],
                                                   sq[s].rearrange("p (c e) n -> p c (e n)", e=2)[:, c, :], ident[:, :])
                            pe_s.done("sq turn", mm)
                            eng.wait_ge(pool_s.sem, pool_s.after("q rope sum", n))
                            eng.wait_ge(dve_s.sem, dve_s.after("kv1", n))
                            for m, row in (("q", qrow), ("k", krow)):
                                for k in range(2):
                                    name = f"{m} turn{k}"
                                    wait_bank_empty(eng, name, n)
                                    for c in range(4):
                                        mm = eng.transpose(bank[bank_of[name]][0:MQ, c * P:(c + 1) * P],
                                                           row[s][:, 4 * k + c, :], ident[:, :])
                                    pe_s.done(name, mm)
                        else:
                            for m in turns:
                                name = m + " turn"
                                who, step = {"qc": (pool_s, "qc"), "kc": (pool_s, "kc"),
                                             "qd": (act_s, "qd"), "kd": (dve_s, "kd")}[m]
                                eng.wait_ge(who.sem, who.after(step, n))
                                wait_bank_empty(eng, name, n)
                                for c in range(4):
                                    mm = eng.transpose(bank[bank_of[name]][:, c * P:(c + 1) * P],
                                                       rows[m][s].rearrange("p (c e) n -> p c (e n)", e=2)[:, c, :],
                                                       ident[:, :])
                                pe_s.done(name, mm)

            def act(eng):
                for s in range(2):
                    eng.sem_inc(rows_out[s], 16)
                with eng.Fori(0, T) as t:
                    for s in range(2):
                        n = t * 2 + s
                        eng.wait_ge(x_in_s[s], t * 32 + 32)
                        eng.wait_ge(pe_s.sem, pe_s.after("h1", n - 2))
                        act_s.done("square", eng.activation(ht[s], xt[s], ACT.Square, accum_out=st[s][:, 0:1]))
                        eng.wait_ge(pe_s.sem, pe_s.after("h0", n))
                        act_s.done("h0", eng.activation(hT[s].rearrange("p a b -> p (a b)")[:, 0:512],
                                                        bank[0][:, :], ACT.Copy))
                        stored = t * 16 * NSTORE + 16
                        if ab:
                            eng.wait_ge(pe_s.sem, pe_s.after("cq", n))
                            act_s.done("cq square", eng.activation(squares_out[s][:, 0:QR], bank[2][:, 0:QR], ACT.Square,
                                                                   accum_out=st[s][:, 3:4]))
                            eng.wait_ge(pe_s.sem, pe_s.after("ckv", n))
                            act_s.done("ckv square", eng.activation(squares_out[s][:, QR:], bank[3][:, 0:KVR],
                                                                    ACT.Square, accum_out=st[s][:, 6:7]))
                            eng.wait_ge(pe_s.sem, pe_s.after("cq turn", n))
                            act_s.done("cq turn", eng.activation(cqT[s].rearrange("p a b -> p (a b)"),
                                                                 bank[6][:, 0:QR], ACT.Copy))
                            eng.wait_ge(rows_out[s], stored)
                            for k in range(2):
                                eng.wait_ge(pe_s.sem, pe_s.after(f"q{k}", n))
                                act_s.done(f"q{k}", eng.activation(
                                    qrow[s][:, 4 * k:4 * k + 4, :].rearrange("p a b -> p (a b)"),
                                    bank[2 + k][:, 0:4 * MQ], ACT.Copy, scale=float(MQ) ** -0.5))
                            eng.wait_ge(pe_s.sem, pe_s.after("sq turn", n))
                            act_s.done("sq turn", eng.activation(sqT[s].rearrange("p a b -> p (a b)"),
                                                                 bank[6][:, :], ACT.Copy))
                            for k in range(2):
                                eng.wait_ge(pe_s.sem, pe_s.after(f"q turn{k}", n))
                                act_s.done(f"q turn{k}", eng.activation(
                                    mqT[s][:, 4 * k:4 * k + 4, :].rearrange("p a b -> p (a b)"),
                                    bank[k][0:MQ, :], ACT.Copy))
                        else:
                            eng.wait_ge(rows_out[s], stored)
                            for m, scale in (("vc", 1.0), ("qd", HD ** -0.5), ("vd", 1.0)):
                                eng.wait_ge(pe_s.sem, pe_s.after(m, n))
                                act_s.done(m, eng.activation(rows[m][s].rearrange("p a b -> p (a b)"),
                                                             bank[bank_of[m]][:, :], ACT.Copy, scale=scale))
                            for m in ("qc", "qd"):
                                eng.wait_ge(pe_s.sem, pe_s.after(m + " turn", n))
                                act_s.done(m + " turn", eng.activation(
                                    turned[m][s].rearrange("p a b -> p (a b)"), bank[bank_of[m + " turn"]][:, :],
                                    ACT.Copy))

            def per_head(table, k, heads):
                return table[:, k:k + 1, :].to_broadcast([P, heads, 64])

            def dve(eng):
                def rope_products(out, out2, src, table, k, heads):
                    eng.tensor_tensor(out, src, per_head(table, k, heads), ALU.mult)
                    eng.tensor_tensor(out2[:, :, 0:32], src[:, :, 32:64], per_head(table, k + 1, heads)[:, :, 0:32], ALU.mult)
                    return eng.tensor_tensor(out2[:, :, 32:64], src[:, :, 0:32],
                                             per_head(table, k + 1, heads)[:, :, 32:64], ALU.mult)

                eng.wait_ge(gain_in, 48 if ab else 16)
                with eng.Fori(0, T) as t:
                    for s in range(2):
                        n = t * 2 + s
                        stored = t * 16 * NSTORE + 16
                        eng.wait_ge(pool_s.sem, pool_s.after("x", n))
                        dve_s.done("h", eng.scalar_tensor_tensor(out=ht[s], in0=xt[s], scalar=st[s][:, 2:3], in1=gain,
                                                                 op0=ALU.mult, op1=ALU.mult))
                        eng.wait_ge(pe_s.sem, pe_s.after("h1", n))
                        dve_s.done("h1", eng.tensor_copy(hT[s].rearrange("p a b -> p (a b)")[:, 512:1024], bank[1][:, :]))
                        if ab:
                            eng.wait_ge(pool_s.sem, pool_s.after("cq", n))
                            dve_s.done("cqn", eng.scalar_tensor_tensor(
                                out=cqn[s].rearrange("p a b -> p (a b)"), in0=bank[2][:, 0:QR], scalar=st[s][:, 5:6],
                                in1=qgain, op0=ALU.mult, op1=ALU.mult))
                            eng.wait_ge(pool_s.sem, pool_s.after("ckv", n))
                            dve_s.done("ckvn", eng.scalar_tensor_tensor(
                                out=ckvn[s].rearrange("p a b -> p (a b)"), in0=bank[3][:, 0:KVR], scalar=st[s][:, 8:9],
                                in1=kvgain, op0=ALU.mult, op1=ALU.mult))
                            dve_s.done("kr", eng.tensor_copy(kr[s][:, 0, :], bank[3][:, KVR:KVR + ROPE]))
                            eng.wait_ge(rows_out[s], stored)
                            eng.wait_ge(pe_s.sem, pe_s.after("qb", n))
                            dve_s.done("qb", rope_products(sq[s], sq2[s], bank[4][:, :].rearrange("p (h d) -> p h d", h=H),
                                                           rt[s], 0, H))
                            eng.wait_ge(pe_s.sem, pe_s.after("kvb", n))
                            v = bank[5][:, KVH * HD:2 * KVH * HD]
                            for g in range(KVH):
                                ins = eng.tensor_copy(
                                    sv[s][:, G * g:G * g + G, :],
                                    v[:, g * HD:(g + 1) * HD].rearrange("p (a d) -> p a d", a=1).to_broadcast([P, G, HD]))
                            dve_s.done("sv", ins)
                            dve_s.done("kvb", rope_products(
                                sk[s], sk2[s], bank[5][:, 0:KVH * HD].rearrange("p (h d) -> p h d", h=KVH), rt[s], 2, KVH))
                            eng.wait_ge(pe_s.sem, pe_s.after("ckv turn", n))
                            dve_s.done("ckv turn", eng.tensor_copy(ckvT[s].rearrange("p a b -> p (a b)"), bank[7][:, 0:KVR]))
                            dve_s.done("sk turn", eng.tensor_copy(skT[s], bank[7][:, KVR:KVR + P]))
                            for k in range(2):
                                eng.wait_ge(pe_s.sem, pe_s.after(f"kv{k}", n))
                                kv = bank[4 + k][:, :].rearrange("p (h d) -> p h d", h=4)
                                eng.tensor_copy(krow[s][:, 4 * k:4 * k + 4, 0:NOPE], kv[:, :, 0:NOPE])
                                dve_s.done(f"kv{k}", eng.tensor_copy(vrow[s][:, 4 * k:4 * k + 4, :], kv[:, :, NOPE:NOPE + MV]))
                            for k in range(2):
                                eng.wait_ge(pe_s.sem, pe_s.after(f"k turn{k}", n))
                                dve_s.done(f"k turn{k}", eng.tensor_copy(
                                    mkT[s][:, 4 * k:4 * k + 4, :].rearrange("p a b -> p (a b)"), bank[2 + k][0:MQ, :]))
                        else:
                            eng.wait_ge(rows_out[s], stored)
                            for m, k in (("qc", 0), ("kc", 2)):
                                eng.wait_ge(pe_s.sem, pe_s.after(m, n))
                                dve_s.done(m, rope_products(rows[m][s], rows2[m][s],
                                                            bank[bank_of[m]][:, :].rearrange("p (h d) -> p h d", h=H),
                                                            rt[s], k, H))
                            eng.wait_ge(pe_s.sem, pe_s.after("kd", n))
                            dve_s.done("kd", eng.tensor_copy(rows["kd"][s].rearrange("p a b -> p (a b)"), bank[6][:, :]))
                            for m in ("kc", "kd"):
                                eng.wait_ge(pe_s.sem, pe_s.after(m + " turn", n))
                                dve_s.done(m + " turn", eng.tensor_copy(
                                    turned[m][s].rearrange("p a b -> p (a b)"), bank[bank_of[m + " turn"]][:, :]))

            def pool(eng):
                def cos(table, k, heads):
                    return table[:, k:k + 1, 0:32].to_broadcast([P, heads, 32])

                def sin(table, k, heads):
                    return table[:, k:k + 1, 32:64].to_broadcast([P, heads, 32])

                def rope32(name, n, src, product, tmp, tmp_rows, table, k, heads, out):
                    lo, hi = slice(0, 16), slice(16, 32)
                    eng.tensor_tensor(tmp[:, tmp_rows, lo], src[:, :, hi], sin(table, k, heads)[:, :, lo], ALU.mult)
                    pool_s.done(name + " a", eng.tensor_tensor(tmp[:, tmp_rows, hi], src[:, :, lo],
                                                               sin(table, k, heads)[:, :, hi], ALU.mult))
                    eng.wait_ge(pool_s.sem, pool_s.after(name + " a", n))
                    pool_s.done(name + " b", eng.tensor_tensor(product, src, cos(table, k, heads), ALU.mult))
                    eng.wait_ge(pool_s.sem, pool_s.after(name + " b", n))
                    pool_s.done(name + " sum", eng.tensor_tensor(
                        out, product.to_broadcast(list(out.shape)), tmp[:, tmp_rows, :].to_broadcast(list(out.shape)), ALU.add))

                with eng.Fori(0, T) as t:
                    for s in range(2):
                        n = t * 2 + s
                        eng.wait_ge(act_s.sem, act_s.after("square", n))
                        rsqrt_mean(eng, pool_s, "x", n, st[s][:, 0:1], st[s][:, 1:2], st[s][:, 2:3], D)
                        if ab:
                            eng.wait_ge(act_s.sem, act_s.after("cq square", n))
                            rsqrt_mean(eng, pool_s, "cq", n, st[s][:, 3:4], st[s][:, 4:5], st[s][:, 5:6], QR)
                            eng.wait_ge(act_s.sem, act_s.after("ckv square", n))
                            rsqrt_mean(eng, pool_s, "ckv", n, st[s][:, 6:7], st[s][:, 7:8], st[s][:, 8:9], KVR)
                            eng.wait_ge(dve_s.sem, dve_s.after("kr", n))
                            eng.wait_ge(pe_s.sem, pe_s.after("k turn1", n - 2))
                            rope32("kr", n, kr[s][:, 0:1, :], kr[s][:, 1:2, :], mtmp[s], slice(H, H + 1), rt[s], 5, 1,
                                   krow[s][:, :, NOPE:MQ])
                            eng.wait_ge(dve_s.sem, dve_s.after("qb", n))
                            pool_s.done("sq", eng.tensor_tensor(sq[s], sq[s], sq2[s], ALU.add))
                            eng.wait_ge(dve_s.sem, dve_s.after("kvb", n))
                            pool_s.done("sk", eng.tensor_tensor(sk[s], sk[s], sk2[s], ALU.add))
                            eng.wait_ge(act_s.sem, act_s.after("q1", n))
                            rope32("q rope", n, qrow[s][:, :, NOPE:MQ], qrow[s][:, :, NOPE:MQ], mtmp[s], slice(0, H), rt[s], 5, H,
                                   qrow[s][:, :, NOPE:MQ])
                        else:
                            for m in ("qc", "kc"):
                                eng.wait_ge(dve_s.sem, dve_s.after(m, n))
                                pool_s.done(m, eng.tensor_tensor(rows[m][s], rows[m][s], rows2[m][s], ALU.add))

            end_stage(sp, pe, act, dve, pool)

        def attention(kind, column, prefetch=None):
            qd, kd, vd = qkv[kind]
            biased = kind != "mla"
            width = P if biased else MQ
            a = Arena()
            q = [a.take(T, 2, P, rows=width) for _ in range(2)]
            k = [a.take(T, 1 if biased else 2, P, rows=width) for _ in range(2)]
            v = [a.take(T, 2 * HD) for _ in range(2)]
            o = [a.take(T, 2 * HD) for _ in range(2)]
            p = [a.take(T, P) for _ in range(4)]
            pT = [a.take(T, P) for _ in range(2)]
            masked = [a.take(T, P) for _ in range(4)] if biased else None
            stat = a.take(4, 16)
            sinks = a.take(2, 2)
            table = a.take(2, SPAN)
            raw = a.take(2, SPAN) if kind == "grid" else None
            column_mask = a.take(GRID_W)
            U = 16
            LAG = 2
            PAIRS = H // 2
            units = [(s, hh, t) for s in range(2) for hh in range(2) for t in range(T)]

            qkv_in = [sem(f"{kind}_qkv_in{s}") for s in range(2)]
            o_out = [sem(f"{kind}_o_out{s}") for s in range(2)]
            table_in = sem(f"{kind}_table_in")
            q_zeroed = sem(f"{kind}_q_zeroed")

            def blocks(t):
                return (max(0, t - 1), min(T, t + 2)) if kind == "window" else (0, T)

            def piped(pieces):
                for i in range(U + LAG + 1):
                    for piece, lag in pieces:
                        if 0 <= i - lag < U:
                            yield piece, i - lag

            PE_PIECES = [("qk", 0), ("turn", LAG), ("pv", LAG + 1)]
            ACT_PIECES = [("turn", LAG), ("exp", 0)]
            DVE_PIECES = [("turn", LAG), ("max", 0), ("recip", LAG), ("out", LAG + 1)]

            pe_s = Steps(counts, "pe", [f"{w}{u}" for w, u in piped(PE_PIECES)], PAIRS)
            act_names = []
            for w, u in piped(ACT_PIECES):
                if w == "exp":
                    act_names.append(f"exp{u}")
                    if kind == "window":
                        act_names.append(f"sink{u}")
                elif u % 2:
                    act_names.append(f"turn{u}")
            act_s = Steps(counts, "act", act_names, PAIRS)
            dve_names = []
            for w, u in piped(DVE_PIECES):
                if w == "recip" and kind == "window":
                    dve_names.append(f"sum{u}")
                if w != "turn" or not u % 2:
                    dve_names.append(f"{w}{u}")
            dve_s = Steps(counts, "dve", dve_names, PAIRS)
            pool_s = Steps(counts, "pool", ["table"], PAIRS) if kind == "grid" else None

            def earlier(u, pair, back):
                return ((u - back) % U, pair if u >= back else pair - 1)

            def wait_unit(eng, steps, step, u, pair, back):
                m, r = earlier(u, pair, back)
                eng.wait_ge(steps.sem, steps.after(f"{step}{m}", r))

            def turner(u):
                return act_s if u % 2 else dve_s

            def sp(eng):
                def load(pair, s):
                    if biased:
                        eng.dma_start(k[s][:, :, 0, :], at(kd, pair * P + T * s * PAIR_TILE,
                                                           [[4 * P, P], [PAIR_TILE, T], [1, P]])).then_inc(qkv_in[s], 16)
                        for e in range(2):
                            eng.dma_start(q[s][64 * e:64 * e + 64, :, e, :],
                                          at(qd, pair * P + T * s * PAIR_TILE + e * HD * 4 * P,
                                             [[4 * P, HD], [PAIR_TILE, T], [1, P]])).then_inc(qkv_in[s], 16)
                    else:
                        w = MQ * H * P
                        for dst, src in ((q, qd), (k, kd)):
                            eng.dma_start(dst[s].rearrange("p t e n -> p t (e n)"),
                                          at(src, pair * (2 * P) + T * s * w, [[H * P, MQ], [w, T], [1, 2 * P]])).then_inc(qkv_in[s], 16)
                    eng.dma_start(v[s], at(vd, pair * (2 * HD) + T * s * P * H * HD,
                                           [[H * HD, P], [P * H * HD, T], [1, 2 * HD]])).then_inc(qkv_in[s], 16)
                    if kind == "window":
                        eng.dma_start(sinks[:, s, :], at(sink, pair * 2, [[0, P], [1, 2]])).then_inc(qkv_in[s], 16)

                def load_bias(pair):
                    eng.dma_start(raw, at(grid_bias, pair * (2 * P * SPAN), [[SPAN, P], [P * SPAN, 2], [1, SPAN]])
                                  ).then_inc(table_in, 16)

                if kind == "window":
                    eng.dma_start(table[:, 0, :], window_table).then_inc(table_in, 16)
                if kind == "dilated":
                    eng.dma_start(table[:, 0, :], dilated_table).then_inc(table_in, 16)
                if kind == "grid":
                    eng.dma_start(column_mask, column_table).then_inc(table_in, 16)
                    load_bias(0)
                if biased:
                    eng.wait_ge(q_zeroed, 2)
                for s in range(2):
                    load(0, s)
                if prefetch:
                    prefetch(eng)

                def store(pair, s):
                    eng.wait_ge(dve_s.sem, dve_s.after(f"out{8 * s + 7}", pair))
                    eng.dma_start(at(mixed, pair * (2 * HD) + T * s * P * D + column, [[D, P], [P * D, T], [1, 2 * HD]]),
                                  o[s]).then_inc(o_out[s], 16)

                with eng.Fori(0, PAIRS - 1) as pair:
                    if kind == "grid":
                        eng.wait_ge(pool_s.sem, pool_s.after("table", pair))
                        load_bias(pair + 1)
                    for s in range(2):
                        store(pair, s)
                        load(pair + 1, s)
                for s in range(2):
                    store(PAIRS - 1, s)
                for s in range(2):
                    eng.wait_ge(o_out[s], 16 * (PAIRS + 1))

            def pe(eng):
                with eng.Fori(0, PAIRS) as pair:
                    for w, u in piped(PE_PIECES):
                        s, e, t = units[u]
                        b0, b1 = blocks(t)
                        if w == "qk":
                            if u % 8 == 0:
                                eng.wait_ge(qkv_in[s], pair * NLOAD + NLOAD)
                            wait_unit(eng, dve_s if biased else act_s, "max" if biased else "exp", u, pair, 4)
                            pe_s.done(f"qk{u}", eng.matmul(
                                bank[u % 4][:, 0:(b1 - b0) * P].rearrange("p (b n) -> p b n", n=P), q[s][:, t, e, :],
                                k[s][:, b0:b1, 0 if biased else e, :], start=True, stop=True))
                        elif w == "turn":
                            wait_unit(eng, act_s, "exp", u, pair, 0)
                            wait_unit(eng, turner(u), "turn", u, pair, 2)
                            for b in range(b1 - b0):
                                mm = eng.transpose(bank[4 + u % 2][:, b * P:(b + 1) * P], p[u % 4][:, b, :], ident[:, :])
                            pe_s.done(f"turn{u}", mm)
                        else:
                            wait_unit(eng, turner(u), "turn", u, pair, 0)
                            wait_unit(eng, dve_s, "out", u, pair, 2)
                            for b in range(b1 - b0):
                                mm = eng.matmul(bank[6 + u % 2][:, 0:HD], pT[u % 2][:, b, :],
                                                v[s][:, b0 + b, e * HD:(e + 1) * HD], start=(b == 0), stop=(b == b1 - b0 - 1))
                            pe_s.done(f"pv{u}", mm)

            NLOAD = 16 * {"mla": 3, "window": 5, "dilated": 4, "grid": 4}[kind]

            def flat(tile, n):
                return tile.rearrange("p a b -> p (a b)")[:, 0:n]

            def act(eng):
                for s in range(2):
                    eng.sem_inc(o_out[s], 16)
                with eng.Fori(0, PAIRS) as pair:
                    for w, u in piped(ACT_PIECES):
                        s, e, t = units[u]
                        b0, b1 = blocks(t)
                        n = (b1 - b0) * P
                        if w == "exp":
                            wait_unit(eng, dve_s, "max", u, pair, 0)
                            wait_unit(eng, pe_s, "turn", u, pair, 4)
                            src = flat(masked[u % 4], n) if biased else bank[u % 4][:, 0:n]
                            act_s.done(f"exp{u}", eng.activation(
                                flat(p[u % 4], n), src, ACT.Exp, bias=stat[:, 0, u:u + 1],
                                scale=-1.0 if biased else 1.0, accum_out=stat[:, 1, u:u + 1]))
                            if kind == "window":
                                act_s.done(f"sink{u}", eng.activation(stat[:, 2, u:u + 1], stat[:, 0, u:u + 1], ACT.Exp,
                                                                      bias=sinks[:, s, e:e + 1], scale=1.0))
                        elif u % 2:
                            wait_unit(eng, pe_s, "turn", u, pair, 0)
                            wait_unit(eng, pe_s, "pv", u, pair, 2)
                            act_s.done(f"turn{u}", eng.activation(flat(pT[u % 2], n), bank[4 + u % 2][:, 0:n], ACT.Copy))

            def dve(eng):
                if biased and kind != "grid":
                    eng.wait_ge(table_in, 16)
                with eng.Fori(0, PAIRS) as pair:
                    if kind == "grid":
                        eng.wait_ge(pool_s.sem, pool_s.after("table", pair))
                    for w, u in piped(DVE_PIECES):
                        s, e, t = units[u]
                        b0, b1 = blocks(t)
                        n = (b1 - b0) * P
                        if w == "max":
                            wait_unit(eng, pe_s, "qk", u, pair, 0)
                            if biased:
                                wait_unit(eng, act_s, "exp", u, pair, 4)
                                c = SEQ - P - P * t + P * b0
                                bias = table[:, e if kind == "grid" else 0, c:c + n]
                                passed(eng)
                                dve_s.done(f"max{u}", eng.tensor_tensor_reduce(
                                    flat(masked[u % 4], n), bank[u % 4][:, 0:n], bias, -1.0, BIG, ALU.add, ALU.min,
                                    stat[:, 0, u:u + 1]))
                            else:
                                dve_s.done(f"max{u}", eng.tensor_reduce(stat[:, 0, u:u + 1], bank[u % 4][:, 0:n], AX.X,
                                                                        ALU.max, negate=True))
                        elif w == "turn":
                            if not u % 2:
                                wait_unit(eng, pe_s, "turn", u, pair, 0)
                                wait_unit(eng, pe_s, "pv", u, pair, 2)
                                dve_s.done(f"turn{u}", eng.tensor_copy(flat(pT[u % 2], n), bank[4 + u % 2][:, 0:n]))
                        elif w == "recip":
                            if kind == "window":
                                wait_unit(eng, act_s, "sink", u, pair, 0)
                                dve_s.done(f"sum{u}", eng.tensor_tensor(stat[:, 1, u:u + 1], stat[:, 1, u:u + 1],
                                                                        stat[:, 2, u:u + 1], ALU.add))
                                wait_unit(eng, dve_s, "sum", u, pair, 0)
                            else:
                                wait_unit(eng, act_s, "exp", u, pair, 0)
                            dve_s.done(f"recip{u}", eng.reciprocal(stat[:, 3, u:u + 1], stat[:, 1, u:u + 1]))
                        else:
                            if u % 8 == 0:
                                eng.wait_ge(o_out[s], pair * 16 + 16)
                            wait_unit(eng, pe_s, "pv", u, pair, 0)
                            wait_unit(eng, dve_s, "recip", u, pair, 0)
                            dve_s.done(f"out{u}", eng.tensor_scalar(o[s][:, t, e * HD:(e + 1) * HD], bank[6 + u % 2][:, 0:HD],
                                                                    stat[:, 3, u:u + 1], None, ALU.mult))

            def pool(eng):
                if biased:
                    for s in range(2):
                        eng.memset(q[s], 0.0).then_inc(q_zeroed, 1)
                if kind != "grid":
                    return
                with eng.Fori(0, PAIRS) as pair:
                    eng.wait_ge(table_in, pair * 16 + 32)
                    wait_unit(eng, dve_s, "max", U - 1, pair - 1, 0)
                    pool_s.done("table", eng.tensor_tensor(
                        table.rearrange("p e (a b) -> p (e a) b", b=GRID_W), raw.rearrange("p e (a b) -> p (e a) b", b=GRID_W),
                        column_mask.rearrange("p (a b) -> p a b", a=1).to_broadcast([P, 28, GRID_W]), ALU.add))

            end_stage(sp, pe, act, dve, pool)

        def output(kind, layer, source, w_out, load_w_out):
            a = Arena()
            gain = a.take(D)
            router = a.take(DC, E)
            ot = [a.take(D) for _ in range(2)]
            xt = [a.take(D) for _ in range(2)]
            oT = [a.take(DC, P) for _ in range(2)]
            xn = [a.take(D) for _ in range(2)]
            h = [a.take(D) for _ in range(2)]
            hT = [a.take(DC, P) for _ in range(2)]
            logits = [a.take(E) for _ in range(2)]
            aff = a.take(48)
            st = [a.take(16) for _ in range(2)]
            wo = ring[:, 4 * PIECE:6 * PIECE].rearrange("p (c n) -> p c n", c=DC)

            const_in = sem(f"{kind}o_const_in")
            rows_in = [sem(f"{kind}o_rows_in{s}") for s in range(2)]
            x_out = [sem(f"{kind}o_x_out{s}") for s in range(2)]
            aff_zero = sem(f"{kind}o_aff_zero")
            pe_s = Steps(counts, "pe", [f"{m}{s}" for m in ("oT0 ", "oT1 ", "y") for s in (0,)] +
                         ["oT0 1", "oT1 1", "y1"] +
                         [f"{m}{s}" for s in range(2) for m in ("hT0 ", "hT1 ", "r")] + ["aff"], T)
            act_s = Steps(counts, "act", ["oT0 0", "oT0 1", "square0", "hT0 0", "square1", "exp0", "hT0 1", "exp1"], T)
            dve_s = Steps(counts, "dve", ["oT1 0", "add0", "oT1 1", "h0", "hT1 0", "add1", "h1", "rmax0", "recip0", "aff0",
                                          "hT1 1", "rmax1", "recip1", "aff1", "aff"], T)
            pool_s = Steps(counts, "pool", [f"x{s}{m}" for s in range(2) for m in (" mean", " eps", "")], T)

            def sp(eng):
                eng.dma_start(gain, at(norm_ffn, layer * D, [[0, P], [1, D]])).then_inc(const_in, 16)
                eng.dma_start(router, at(w_router, layer * D * E, [[E, P], [P * E, DC], [1, E]])).then_inc(const_in, 16)
                if load_w_out:
                    eng.dma_start(wo, w_out.rearrange("(c p) n -> p c n", p=P)).then_inc(const_in, 16)

                def load(t, s):
                    tile = [[D, P], [1, D]]
                    eng.dma_start(ot[s], at(mixed, (t + T * s) * P * D, tile)).then_inc(rows_in[s], 16)
                    eng.dma_start(xt[s], at(source, (t + T * s) * P * D, tile)).then_inc(rows_in[s], 16)

                def store(t, s):
                    tile = [[D, P], [1, D]]
                    eng.wait_ge(dve_s.sem, dve_s.after(f"add{s}", t))
                    eng.dma_start(at(residual, (t + T * s) * P * D, tile), xn[s]).then_inc(x_out[s], 16)
                    eng.wait_ge(dve_s.sem, dve_s.after(f"h{s}", t))
                    eng.dma_start(at(normed, (t + T * s) * P * D, tile), h[s]).then_inc(x_out[s], 16)

                for s in range(2):
                    load(0, s)
                with eng.Fori(0, T - 1) as t:
                    for s in range(2):
                        store(t, s)
                        load(t + 1, s)
                for s in range(2):
                    store(T - 1, s)
                for s in range(2):
                    eng.wait_ge(x_out[s], 32 * (T + 1))

            def pe(eng):
                eng.wait_ge(const_in, 48)
                with eng.Fori(0, T) as t:
                    for s in range(2):
                        eng.wait_ge(rows_in[s], t * 32 + 32)
                        for k in range(2):
                            who = act_s if k == 0 else dve_s
                            eng.wait_ge(who.sem, who.after(f"oT{k} {1 - s}", t if s else t - 1))
                            for c in range(4):
                                mm = eng.transpose(bank[k][:, c * P:(c + 1) * P],
                                                   ot[s][:, (4 * k + c) * P:(4 * k + c + 1) * P], ident[:, :])
                            pe_s.done(f"oT{k} {s}", mm)
                        eng.wait_ge(act_s.sem, act_s.after(f"oT0 {s}", t))
                        eng.wait_ge(dve_s.sem, dve_s.after(f"oT1 {s}", t))
                        eng.wait_ge(dve_s.sem, dve_s.after(f"add{1 - s}", t if s else t - 1))
                        for c in range(DC):
                            for k in range(2):
                                mm = eng.matmul(bank[2 + k][:, :], oT[s][:, c, :], wo[:, c, k * BANK:(k + 1) * BANK],
                                                start=(c == 0), stop=(c == DC - 1))
                        pe_s.done(f"y{s}", mm)
                    for s in range(2):
                        eng.wait_ge(dve_s.sem, dve_s.after(f"h{s}", t))
                        for k in range(2):
                            who = act_s if k == 0 else dve_s
                            eng.wait_ge(who.sem, who.after(f"hT{k} {1 - s}", t if s else t - 1))
                            for c in range(4):
                                mm = eng.transpose(bank[4 + k][:, c * P:(c + 1) * P],
                                                   h[s][:, (4 * k + c) * P:(4 * k + c + 1) * P], ident[:, :])
                            pe_s.done(f"hT{k} {s}", mm)
                        eng.wait_ge(act_s.sem, act_s.after(f"hT0 {s}", t))
                        eng.wait_ge(dve_s.sem, dve_s.after(f"hT1 {s}", t))
                        eng.wait_ge(act_s.sem, act_s.after(f"exp{1 - s}", t if s else t - 1))
                        for c in range(DC):
                            mm = eng.matmul(bank[6][:, 0:E], hT[s][:, c, :], router[:, c, :],
                                            start=(c == 0), stop=(c == DC - 1))
                        pe_s.done(f"r{s}", mm)
                    eng.wait_ge(dve_s.sem, dve_s.after("aff1", t))
                    passed(eng)
                    pe_s.done("aff", eng.transpose(bank[7][0:48, 0:P], aff, ident[:, :]))

            def act(eng):
                for s in range(2):
                    eng.sem_inc(x_out[s], 32)
                with eng.Fori(0, T) as t:
                    def turn(s):
                        eng.wait_ge(pe_s.sem, pe_s.after(f"oT0 {s}", t))
                        act_s.done(f"oT0 {s}", eng.activation(oT[s].rearrange("p a b -> p (a b)")[:, 0:512], bank[0][:, :], ACT.Copy))

                    def square(s):
                        eng.wait_ge(dve_s.sem, dve_s.after(f"add{s}", t))
                        eng.wait_ge(pe_s.sem, pe_s.after(f"r{s}", t - 1))
                        act_s.done(f"square{s}", eng.activation(hT[s].rearrange("p a b -> p (a b)"), xn[s], ACT.Square,
                                                                accum_out=st[s][:, 0:1]))

                    def turn_h(s):
                        eng.wait_ge(pe_s.sem, pe_s.after(f"hT0 {s}", t))
                        act_s.done(f"hT0 {s}", eng.activation(hT[s].rearrange("p a b -> p (a b)")[:, 0:512], bank[4][:, :], ACT.Copy))

                    def exp(s):
                        eng.wait_ge(dve_s.sem, dve_s.after(f"rmax{s}", t))
                        act_s.done(f"exp{s}", eng.activation(logits[s], bank[6][:, 0:E], ACT.Exp, bias=st[s][:, 3:4],
                                                             scale=1.0, accum_out=st[s][:, 4:5]))
                    turn(0)
                    turn(1)
                    square(0)
                    turn_h(0)
                    square(1)
                    exp(0)
                    turn_h(1)
                    exp(1)

            def dve(eng):
                eng.memset(aff, 0.0).then_inc(aff_zero, 1)
                eng.wait_ge(aff_zero, 1)
                eng.wait_ge(const_in, 48)
                with eng.Fori(0, T) as t:
                    def turn(s):
                        eng.wait_ge(pe_s.sem, pe_s.after(f"oT1 {s}", t))
                        dve_s.done(f"oT1 {s}", eng.tensor_copy(oT[s].rearrange("p a b -> p (a b)")[:, 512:1024], bank[1][:, :]))

                    def add(s):
                        eng.wait_ge(pe_s.sem, pe_s.after(f"y{s}", t))
                        eng.wait_ge(x_out[s], t * 32 + 32)
                        eng.tensor_tensor(xn[s][:, 0:512], bank[2][:, :], xt[s][:, 0:512], ALU.add)
                        dve_s.done(f"add{s}", eng.tensor_tensor(xn[s][:, 512:1024], bank[3][:, :], xt[s][:, 512:1024], ALU.add))

                    def norm(s):
                        eng.wait_ge(pool_s.sem, pool_s.after(f"x{s}", t))
                        dve_s.done(f"h{s}", eng.scalar_tensor_tensor(out=h[s], in0=xn[s], scalar=st[s][:, 2:3], in1=gain,
                                                                     op0=ALU.mult, op1=ALU.mult))

                    def turn_h(s):
                        eng.wait_ge(pe_s.sem, pe_s.after(f"hT1 {s}", t))
                        dve_s.done(f"hT1 {s}", eng.tensor_copy(hT[s].rearrange("p a b -> p (a b)")[:, 512:1024], bank[5][:, :]))

                    def softmax(s):
                        eng.wait_ge(pe_s.sem, pe_s.after(f"r{s}", t))
                        dve_s.done(f"rmax{s}", eng.tensor_reduce(st[s][:, 3:4], bank[6][:, 0:E], AX.X, ALU.max, negate=True))
                        eng.wait_ge(act_s.sem, act_s.after(f"exp{s}", t))
                        dve_s.done(f"recip{s}", eng.reciprocal(st[s][:, 5:6], st[s][:, 4:5]))
                        eng.wait_ge(dve_s.sem, dve_s.after(f"recip{s}", t))
                        if s == 0:
                            eng.wait_ge(pe_s.sem, pe_s.after("aff", t - 1))
                        dve_s.done(f"aff{s}", eng.tensor_scalar(aff[:, 32 * s:32 * s + E], logits[s], st[s][:, 5:6], None, ALU.mult))
                    turn(0)
                    add(0)
                    turn(1)
                    norm(0)
                    turn_h(0)
                    add(1)
                    norm(1)
                    softmax(0)
                    turn_h(1)
                    softmax(1)
                    eng.wait_ge(pe_s.sem, pe_s.after("aff", t))
                    dve_s.done("aff", eng.tensor_scalar(aff_turned[:, bass.ds(t * P, P)], bank[7][0:48, 0:P], 1.0, None, ALU.mult))

            def pool(eng):
                with eng.Fori(0, T) as t:
                    for s in range(2):
                        eng.wait_ge(act_s.sem, act_s.after(f"square{s}", t))
                        rsqrt_mean(eng, pool_s, f"x{s}", t, st[s][:, 0:1], st[s][:, 1:2], st[s][:, 2:3], D)

            end_stage(sp, pe, act, dve, pool)

        def choose(kind):
            a = Arena()
            best = a.take(CAP, rows=48)
            where_u = a.take(CAP, rows=48).bitcast(U32)
            spread_i = a.take(P, rows=48)
            spread_v = a.take(P, rows=48)
            ROUNDS = CAP // 8
            zeroed = sem(f"{kind}_zeroed")
            names = []
            for r in range(ROUNDS):
                names += [f"max{r}", f"index{r}", f"replace{r}"]
            dve_s = Steps(counts, "dve", names + ["spread", "chosen"], 1)
            pe_s = Steps(counts, "pe", ["slots"], 1)

            def sp(eng):
                pass

            def act(eng):
                pass

            def pe(eng):
                eng.wait_ge(dve_s.sem, dve_s.after("spread"))
                eng.matmul(bank[0][:, 0:E], spread_i, rows_to_slots[:, :], start=True, stop=True)
                pe_s.done("slots", eng.matmul(bank[1][:, 0:E], spread_v, rows_to_slots[:, :], start=True, stop=True))

            def dve(eng):
                for r in range(ROUNDS):
                    c = slice(8 * r, 8 * r + 8)
                    if r:
                        eng.wait_ge(dve_s.sem, dve_s.after(f"replace{r - 1}"))
                    dve_s.done(f"max{r}", eng.max(best[:, c], aff_turned[:, :]))
                    eng.wait_ge(dve_s.sem, dve_s.after(f"max{r}"))
                    dve_s.done(f"index{r}", eng.max_index(where_u[:, c], best[:, c], aff_turned[:, :]))
                    dve_s.done(f"replace{r}", eng.match_replace(aff_turned[:, :], best[:, c], aff_turned[:, :], -1.0))
                eng.wait_ge(zeroed, 2)
                eng.wait_ge(dve_s.sem, dve_s.after(f"index{ROUNDS - 1}"))
                eng.tensor_copy(spread_i[0:16, 0:CAP], where_u[0:16, :])
                eng.tensor_scalar(spread_i[32:48, CAP:P], where_u[32:48, :], float(SEQ), None, ALU.add)
                eng.tensor_copy(spread_v[0:16, 0:CAP], best[0:16, :])
                dve_s.done("spread", eng.tensor_copy(spread_v[32:48, CAP:P], best[32:48, :]))
                eng.wait_ge(pe_s.sem, pe_s.after("slots"))
                eng.wait_ge(zeroed, 3)
                eng.tensor_copy(chosen[:, 0:E], bank[0][:, 0:E])
                dve_s.done("chosen", eng.tensor_copy(gates[:, 0:E], bank[1][:, 0:E]))

            def pool(eng):
                eng.memset(spread_i, 0.0).then_inc(zeroed, 1)
                eng.memset(spread_v, 0.0).then_inc(zeroed, 1)
                eng.memset(chosen[:, :].bitcast(F32), 0.0).then_inc(zeroed, 1)

            end_stage(sp, pe, act, dve, pool)

        SOURCES = [(w_gate, 0), (w_gate, 1), (w_up, 0), (w_up, 1), (w_down, 0), (w_down, 1)]

        def load_piece(eng, layer, e, k):
            w, half = SOURCES[k]
            eng.dma_start(ring[:, k * PIECE:(k + 1) * PIECE].rearrange("p (c n) -> p c n", c=4),
                          at(w, (e + layer * E) * (D * F) + half * (D * F // 2), [[F, P], [P * F, 4], [1, F]])
                          ).then_inc(piece_in[k], 16)

        def experts(layer):
            a = Arena()
            rows = [a.take(D) for _ in range(2)]
            xT = [a.take(DC, P) for _ in range(2)]
            sig = a.take(F)
            gated = a.take(F)
            hidden = a.take(F)
            hT = a.take(DC, P)
            y = [a.take(D) for _ in range(2)]
            index = [a.take(1).bitcast(U32) for _ in range(2)]
            gate = [a.take(1) for _ in range(2)]
            piece = [ring[:, k * PIECE:(k + 1) * PIECE].rearrange("p (c n) -> p c n", c=4) for k in range(RING)]
            rows_in = [sem(f"rows_in{layer}{j}") for j in range(2)]
            scattered = sem(f"scattered{layer}")
            before = list(pieces)

            pe_names = ["gate lo", "gate hi", "up0", "up1", "x0", "x1", "h0", "h1", "down lo", "down hi"]
            act_names = ["exp0", "exp1", "x0", "h0", "y0"]
            dve_names = ["den0", "sig0", "silu0", "den1", "sig1", "silu1", "hidden0", "hidden1", "x1", "h1", "y1"]
            pool_names = ["index", "gate"]
            pe_s = Steps(counts, "pe", pe_names, E, lead=6)
            act_s = Steps(counts, "act", act_names, E, lead=3)
            dve_s = Steps(counts, "dve", dve_names, E, lead=3)
            pool_s = Steps(counts, "pool", pool_names, E + 1)
            freed = ["gate lo", "gate hi", "up1", "up1", "down lo", "down hi"]

            def sp(eng):
                load_piece(eng, layer, 0, 4)
                load_piece(eng, layer, 0, 5)
                with eng.Fori(1, E) as e:
                    for k in range(RING):
                        eng.wait_ge(pe_s.sem, pe_s.after(freed[k], e - 1))
                        load_piece(eng, layer, e, k)

            def turn_rows(eng, j, k, done):
                for c in range(4):
                    mm = eng.transpose(bank[k][:, c * P:(c + 1) * P],
                                       rows[j][:, (4 * k + c) * P:(4 * k + c + 1) * P], ident[:, :])
                done(mm)

            def pe(eng):
                eng.wait_ge(rows_in[0], 16)
                turn_rows(eng, 0, 0, lambda mm: mm.then_inc(pe_s.sem, 1))
                turn_rows(eng, 0, 1, lambda mm: mm.then_inc(pe_s.sem, 5))
                with eng.Fori(0, E // 2) as pair:
                    for j in range(2):
                        e = pair * 2 + j
                        landed = lambda k: eng.wait_ge(piece_in[k], e * 16 + (16 * before[k] + 16))
                        eng.wait_ge(act_s.sem, act_s.after("x0", e - 1))
                        eng.wait_ge(dve_s.sem, dve_s.after("x1", e - 1))
                        for half, name in ((0, "gate lo"), (1, "gate hi")):
                            landed(half)
                            for c in range(4):
                                for k in range(2):
                                    mm = eng.matmul(bank[2 + k][:, :], xT[j][:, 4 * half + c, :],
                                                    piece[half][:, c, k * BANK:(k + 1) * BANK],
                                                    start=(half == 0 and c == 0), stop=(half == 1 and c == 3))
                            pe_s.done(name, mm)
                        landed(2)
                        landed(3)
                        for k in range(2):
                            eng.wait_ge(dve_s.sem, dve_s.after(f"hidden{k}", e - 1))
                            for c in range(DC):
                                mm = eng.matmul(bank[4 + k][:, :], xT[j][:, c, :],
                                                piece[2 + c // 4][:, c % 4, k * BANK:(k + 1) * BANK],
                                                start=(c == 0), stop=(c == DC - 1))
                            pe_s.done(f"up{k}", mm)
                        eng.wait_ge(rows_in[1 - j], pair * 16 + (32 if j else 16))
                        for k in range(2):
                            turn_rows(eng, 1 - j, k, lambda mm: pe_s.done(f"x{k}", mm))
                        for k in range(2):
                            eng.wait_ge(dve_s.sem, dve_s.after(f"hidden{k}", e))
                            for c in range(4):
                                mm = eng.transpose(bank[2 + k][:, c * P:(c + 1) * P],
                                                   hidden[:, (4 * k + c) * P:(4 * k + c + 1) * P], ident[:, :])
                            pe_s.done(f"h{k}", mm)
                        eng.wait_ge(act_s.sem, act_s.after("y0", e - 1))
                        eng.wait_ge(dve_s.sem, dve_s.after("y1", e - 1))
                        for half, name in ((0, "down lo"), (1, "down hi")):
                            landed(4 + half)
                            who = dve_s if half else act_s
                            eng.wait_ge(who.sem, who.after(f"h{half}", e))
                            for c in range(4):
                                for k in range(2):
                                    mm = eng.matmul(bank[6 + k][:, :], hT[:, 4 * half + c, :],
                                                    piece[4 + half][:, c, k * BANK:(k + 1) * BANK],
                                                    start=(half == 0 and c == 0), stop=(half == 1 and c == 3))
                            pe_s.done(name, mm)

            def act(eng):
                def take_x(j):
                    return eng.activation(xT[j].rearrange("p a b -> p (a b)")[:, 0:512], bank[0][:, :], ACT.Copy)

                eng.wait_ge(pe_s.sem, pe_s.after("x0", -1))
                take_x(0).then_inc(act_s.sem, 3)
                with eng.Fori(0, E // 2) as pair:
                    for j in range(2):
                        e = pair * 2 + j
                        eng.wait_ge(pe_s.sem, pe_s.after("gate hi", e))
                        for k in range(2):
                            eng.wait_ge(dve_s.sem, dve_s.after(f"silu{k}", e - 1))
                            act_s.done(f"exp{k}", eng.activation(sig[:, k * 512:(k + 1) * 512], bank[2 + k][:, :], ACT.Exp, scale=-1.0))
                        eng.wait_ge(pe_s.sem, pe_s.after("x0", e))
                        act_s.done("x0", take_x(1 - j))
                        eng.wait_ge(pe_s.sem, pe_s.after("h0", e))
                        act_s.done("h0", eng.activation(hT.rearrange("p a b -> p (a b)")[:, 0:512], bank[2][:, :], ACT.Copy))
                        eng.wait_ge(pe_s.sem, pe_s.after("down hi", e))
                        eng.wait_ge(pool_s.sem, pool_s.after("gate", e))
                        act_s.done("y0", eng.activation(y[j][:, 0:512], bank[6][:, :], ACT.Copy, scale=gate[j]))

            def dve(eng):
                def take_x(j):
                    return eng.tensor_copy(xT[j].rearrange("p a b -> p (a b)")[:, 512:1024], bank[1][:, :])

                eng.wait_ge(pe_s.sem, pe_s.after("x1", -1))
                take_x(0).then_inc(dve_s.sem, 3)
                with eng.Fori(0, E // 2) as pair:
                    for j in range(2):
                        e = pair * 2 + j
                        for k in range(2):
                            half = slice(k * 512, (k + 1) * 512)
                            eng.wait_ge(act_s.sem, act_s.after(f"exp{k}", e))
                            dve_s.done(f"den{k}", eng.tensor_scalar(sig[:, half], sig[:, half], 1.0, None, ALU.add))
                            eng.wait_ge(dve_s.sem, dve_s.after(f"den{k}", e))
                            dve_s.done(f"sig{k}", eng.reciprocal(sig[:, half], sig[:, half]))
                            eng.wait_ge(dve_s.sem, dve_s.after(f"sig{k}", e))
                            dve_s.done(f"silu{k}", eng.tensor_tensor(gated[:, half], bank[2 + k][:, :], sig[:, half], ALU.mult))
                        for k in range(2):
                            half = slice(k * 512, (k + 1) * 512)
                            eng.wait_ge(pe_s.sem, pe_s.after(f"up{k}", e))
                            eng.wait_ge(dve_s.sem, dve_s.after(f"silu{k}", e))
                            dve_s.done(f"hidden{k}", eng.tensor_tensor(hidden[:, half], bank[4 + k][:, :], gated[:, half], ALU.mult))
                        eng.wait_ge(pe_s.sem, pe_s.after("x1", e))
                        dve_s.done("x1", take_x(1 - j))
                        eng.wait_ge(pe_s.sem, pe_s.after("h1", e))
                        dve_s.done("h1", eng.tensor_copy(hT.rearrange("p a b -> p (a b)")[:, 512:1024], bank[3][:, :]))
                        eng.wait_ge(pe_s.sem, pe_s.after("down hi", e))
                        eng.wait_ge(pool_s.sem, pool_s.after("gate", e))
                        dve_s.done("y1", eng.tensor_scalar(y[j][:, 512:1024], bank[7][:, :], gate[j], None, ALU.mult))

            def pool(eng):
                def gather(e, j, n):
                    passed(eng)
                    pool_s.done("index", eng.tensor_copy(index[j], chosen[:, e]))
                    pool_s.done("gate", eng.tensor_copy(gate[j], gates[:, e]))
                    eng.wait_ge(pool_s.sem, pool_s.after("index", n))
                    eng.wait_ge(pe_s.sem, pe_s.after("x1", n - 2))
                    passed(eng)
                    eng.indirect_dma_start(out=rows[j], out_offset=None, in_=normed,
                                           in_offset=bass.IndirectOffsetOnAxis(ap=index[j], axis=0)).then_inc(rows_in[j], 16)

                gather(slice(0, 1), 0, 0)
                with eng.Fori(0, E // 2) as pair:
                    for j in range(2):
                        e = pair * 2 + j
                        if j:
                            eng.wait_ge(scattered, pair * 32 + 16)
                        gather(bass.ds(e + 1, 1), 1 - j, e + 1)
                        eng.wait_ge(act_s.sem, act_s.after("y0", e))
                        eng.wait_ge(dve_s.sem, dve_s.after("y1", e))
                        passed(eng)
                        eng.indirect_dma_start(out=residual, out_offset=bass.IndirectOffsetOnAxis(ap=index[j], axis=0),
                                               in_=y[j], in_offset=None, compute_op=ALU.add).then_inc(scattered, 16)
                    eng.wait_ge(scattered, pair * 32 + 32)
                eng.wait_ge(rows_in[0], 16 * (E // 2 + 1))

            for k in range(RING):
                pieces[k] += E
            end_stage(sp, pe, act, dve, pool)

        def finish():
            a = Arena()
            gain = a.take(D)
            xt = [a.take(D) for _ in range(2)]
            sq = [a.take(D) for _ in range(2)]
            yt = [a.take(D) for _ in range(2)]
            st = [a.take(4) for _ in range(2)]
            gain_in = sem("final_gain_in")
            rows_in = [sem(f"final_rows_in{s}") for s in range(2)]
            y_stored = [sem(f"y_stored{s}") for s in range(2)]
            act_s = Steps(counts, "act", ["square0", "square1"], T)
            pool_s = Steps(counts, "pool", [f"x{s}{m}" for s in range(2) for m in (" mean", " eps", "")], T)
            dve_s = Steps(counts, "dve", ["y0", "y1"], T)

            def sp(eng):
                tile = [[D, P], [1, D]]

                def load(t, s):
                    eng.dma_start(xt[s], at(residual, (t + T * s) * P * D, tile)).then_inc(rows_in[s], 16)

                def store(t, s):
                    eng.wait_ge(dve_s.sem, dve_s.after(f"y{s}", t))
                    eng.dma_start(at(y_out, (t + T * s) * P * D, tile), yt[s]).then_inc(y_stored[s], 16)
                eng.dma_start(gain, at(norm_final, 0, [[0, P], [1, D]])).then_inc(gain_in, 16)
                load(0, 0)
                load(0, 1)
                with eng.Fori(0, T - 1) as t:
                    for s in range(2):
                        store(t, s)
                        load(t + 1, s)
                for s in range(2):
                    store(T - 1, s)
                for s in range(2):
                    eng.wait_ge(y_stored[s], 16 * (T + 1))

            def pe(eng):
                pass

            def act(eng):
                for s in range(2):
                    eng.sem_inc(y_stored[s], 16)
                with eng.Fori(0, T) as t:
                    for s in range(2):
                        eng.wait_ge(rows_in[s], t * 16 + 16)
                        act_s.done(f"square{s}", eng.activation(sq[s], xt[s], ACT.Square, accum_out=st[s][:, 0:1]))

            def pool(eng):
                with eng.Fori(0, T) as t:
                    for s in range(2):
                        eng.wait_ge(act_s.sem, act_s.after(f"square{s}", t))
                        rsqrt_mean(eng, pool_s, f"x{s}", t, st[s][:, 0:1], st[s][:, 1:2], st[s][:, 2:3], D)

            def dve(eng):
                eng.wait_ge(gain_in, 16)
                with eng.Fori(0, T) as t:
                    for s in range(2):
                        eng.wait_ge(pool_s.sem, pool_s.after(f"x{s}", t))
                        eng.wait_ge(y_stored[s], t * 16 + 16)
                        dve_s.done(f"y{s}", eng.scalar_tensor_tensor(out=yt[s], in0=xt[s], scalar=st[s][:, 2:3], in1=gain,
                                                                     op0=ALU.mult, op1=ALU.mult))

            end_stage(sp, pe, act, dve, pool)

        wo_ring = ring[:, 4 * PIECE:6 * PIECE].rearrange("p (c n) -> p c n", c=DC)
        w_out_in = sem("w_out_in")

        def first_pieces(layer):
            def prefetch(eng):
                for k in range(4):
                    load_piece(eng, layer, 0, k)
            return prefetch

        plan = [start,
                lambda: project("ab", 0, x_in),
                lambda: attention("mla", 0),
                lambda: attention("window", H * MV, prefetch=first_pieces(0)),
                lambda: output("ab", 0, x_in, w_out_ab, True),
                lambda: choose("ab"),
                lambda: experts(0),
                lambda: project("cd", 1, residual),
                lambda: attention("dilated", 0),
                lambda: attention("grid", H * HD, prefetch=first_pieces(1)),
                lambda: output("cd", 1, residual, w_out_cd, True),
                lambda: choose("cd"),
                lambda: experts(1),
                finish]
        for stage in plan:
            stage()

        with nc.Block() as block:
            @block.sync
            def _(eng):
                for program in block_programs["sp"]:
                    program(eng)

            @block.tensor
            def _(eng):
                for program in block_programs["pe"]:
                    program(eng)

            @block.scalar
            def _(eng):
                for program in block_programs["act"]:
                    program(eng)

            @block.vector
            def _(eng):
                for program in block_programs["dve"]:
                    program(eng)

            @block.gpsimd
            def _(eng):
                for program in block_programs["pool"]:
                    program(eng)


def rope_rows():
    import numpy as np

    def angles(dim):
        inv = (1.0 / (np.float32(10000.0) ** (np.arange(0, dim, 2, dtype=np.float32) / dim))).astype(np.float32)
        a = (np.arange(SEQ, dtype=np.float32)[:, None] * inv[None, :]).astype(np.float64)
        return np.cos(a).astype(np.float32), np.sin(a).astype(np.float32)
    c, s = angles(HD)
    cos, sin = np.concatenate([c, c], 1), np.concatenate([-s, s], 1)
    scale = np.float32(HD ** -0.5)
    c, s = angles(ROPE)
    small = np.concatenate([c, c, -s, s], 1)
    return np.ascontiguousarray(np.concatenate([cos * scale, sin * scale, cos, sin, small, small], 1).astype(np.float32))


def key_tables():
    import numpy as np
    d = np.arange(SPAN)[None, :] - (SEQ - P) - np.arange(P)[:, None]
    window = np.where(np.abs(d) <= 128, 0.0, NEG).astype(np.float32)
    times = (np.abs(d) <= 64).astype(int) + ((d % 4 == 0) & (np.abs(d) <= 256)) + (d % 16 == 0)
    dilated = np.where(times > 0, np.log(np.maximum(times, 1)), NEG).astype(np.float32)
    c = np.arange(P)[:, None] % GRID_W
    first = np.clip(c - 8, 0, GRID_W - 16)
    k = np.arange(GRID_W)[None, :]
    columns = np.where((k >= first) & (k < first + 16), 0.0, NEG).astype(np.float32)
    return window, dilated, columns


def host_arrays(inputs):
    import numpy as np
    g = {n: np.asarray(a) for n, a in inputs.items()}
    window, dilated, columns = key_tables()
    return {
        "x_in": np.concatenate([g["x_prompt"][0], g["x_sample"][0]], 0),
        "norm_mix": g["norm_mix"], "norm_ffn": g["norm_ffn"], "norm_final": g["norm_final"],
        "w_in_ab": g["w_in_ab"][0], "q_norm": g["mla_q_norm"], "w_uq": g["mla_w_uq"][0],
        "kv_norm": g["mla_kv_norm"], "w_ukv": g["mla_w_ukv"][0], "sink": g["swa_sink"],
        "w_out_ab": g["w_out_ab"][0], "w_in_cd": g["w_in_cd"][0],
        "rpb_padded": np.pad(g["na_rpb"][0], ((0, 0), (0, 0), (48, P - 48 - 31))),
        "w_out_cd": g["w_out_cd"][0], "w_router": g["w_router"], "w_gate": g["w_gate"],
        "w_up": g["w_up"], "w_down": g["w_down"],
        "rope_table": rope_rows(), "window_table": window, "dilated_table": dilated, "column_table": columns,
    }


def kernel(**inputs):
    import numpy as _np
    import concourse.bacc as _bacc
    from concourse import mybir as _mybir
    from concourse.bass_utils import run_bass_kernel_spmd as _run

    nc = _bacc.Bacc("TRN2", target_bir_lowering=False, num_devices=1)
    arrays, args = {}, {}
    for name, a in host_arrays(inputs).items():
        a = _np.ascontiguousarray(a)
        arrays[f"in_{name}"] = a
        args[name] = nc.dram_tensor(f"in_{name}", a.shape, _mybir.dt.from_np(a.dtype), kind="ExternalInput").ap()
    args["y_out"] = nc.dram_tensor("y_out", (TOK, D), _mybir.dt.float32, kind="ExternalOutput").ap()
    hybrid_trunk(nc, **args)
    r = _run(nc, [arrays], core_ids=[0])
    y = r.results[0]["y_out"]
    return y[None, 0:SEQ], y[None, SEQ:TOK]
```

```python
from contextlib import ExitStack

import concourse.bass as bass
from concourse import mybir

F32 = mybir.dt.float32
U32 = mybir.dt.uint32
ALU = mybir.AluOpType
ACT = mybir.ActivationFunctionType
AX = mybir.AxisListType

P = 128
D = 1024
SEQ = 512
SEQS = 2
T = SEQ // P
TOK = SEQS * SEQ
DC = D // P
BANK = 512
EPS = 1e-6
NEG = -1e30
BIG = 3e38

QR, KVR, ROPE, NOPE, MV = 384, 256, 32, 64, 64
H = 8
HD = 64
KVH = 2
G = H // KVH
MQ = NOPE + ROPE
AB_IN = QR + KVR + ROPE + (H + 2 * KVH) * HD
SPAN = 2 * SEQ - P
E = 16
CAP = 64
F = 1024
GRID_W = 64
CREDIT = 256


class Steps:

    def __init__(self, counts, engine, names, rounds, lead=0, lags={}):
        self.sem, start = counts[engine]
        self.base = start + lead
        self.index = {name: k for k, name in enumerate(names)}
        self.names, self.lags = list(names), lags
        self.per = len(names)
        assert len(self.index) == self.per
        counts[engine] = (self.sem, self.base + self.per * rounds)
        self.told = 0
        self.part()

    def after(self, name, n=0):
        return n * self.per + (self.base + self.lags.get(name, 0) * self.per + self.index[name] + 1)

    def skip(self, n):
        self.told += n

    def part(self, left_out=()):
        self.left_out = left_out

    def finish(self, eng):
        rest = -self.told % self.per if self.told % self.per else (0 if set(self.names) - set(self.left_out) else self.per)
        if rest:
            eng.drain().then_inc(self.sem, rest)

    def done(self, name, instruction):
        step = 1
        while self.names[self.told % self.per] != name:
            assert self.names[self.told % self.per] in self.left_out, name
            self.told += 1
            step += 1
        self.told += 1
        while self.told % self.per and self.names[self.told % self.per] in self.left_out:
            self.told += 1
            step += 1
        instruction.then_inc(self.sem, step)


def hybrid_trunk(nc, x_in, norm_mix, norm_ffn, norm_final, w_in_ab, q_norm, w_uq, kv_norm, w_ukv, sink,
                 w_out_ab, w_in_cd, rpb_padded, w_out_cd, w_router, w_gate, w_up, w_down,
                 rope_table, window_table, dilated_table, column_table, y_out):
    with ExitStack() as ctx:
        def sb(name, shape, dt=F32):
            return ctx.enter_context(nc.sbuf_tensor(name, shape, dt))

        def sem(name):
            return ctx.enter_context(nc.semaphore(name))

        def dram(name, shape):
            return nc.dram_tensor(name, shape, F32, kind="Internal").ap()

        def at(a, offset, pattern):
            return bass.AP(a.tensor, offset, pattern)

        WIDTHS = (D, QR, KVR)
        RING = 6
        PIECE = 4 * 1024
        ring = sb("ring", [P, RING * PIECE])
        ARENA = 27136
        arena = sb("arena", [P, ARENA])
        ident = sb("ident", [P, P])
        minus_half = sb("minus_half", [P, 1])
        epsilon = sb("epsilon", [P, 1])
        one_over = sb("one_over", [P, 3])
        rows_to_slots = sb("rows_to_slots", [48, E])
        aff_turned = sb("aff_turned", [48, SEQ])
        chosen = sb("chosen", [P, E + 1], U32)
        gates = sb("gates", [P, E + 1])
        bank = [ctx.enter_context(nc.psum_tensor(f"bank{b}", [P, BANK], F32)) for b in range(8)]

        class Arena:
            def __init__(self, start=0, memory=None, end=ARENA):
                self.at, self.end = start, end
                self.memory = arena if memory is None else memory

            def take(self, *shape, rows=P):
                n = 1
                for k in shape:
                    n *= k
                v = self.memory[0:rows, self.at:self.at + n]
                self.at += n
                assert self.at <= self.end, self.at
                if len(shape) == 1:
                    return v
                letters = "abcd"[:len(shape)]
                sizes = dict(zip(letters, shape))
                return v.rearrange(f"p ({' '.join(letters)}) -> p {' '.join(letters)}", **sizes)

        residual = dram("residual", [TOK, D])
        normed = dram("normed", [TOK, D])
        mixed = dram("mixed", [TOK, D])
        grid_bias = dram("grid_bias", [H, P, SPAN])
        qkv = {kind: (dram(f"q_{kind}", [8, w, n * P]), dram(f"k_{kind}", [8, w, n * P]),
                      dram(f"v_{kind}", [8, P, H * HD]))
               for kind, w, n in (("mla", MQ, H), ("window", P, H // 2), ("dilated", P, H // 2), ("grid", P, H // 2))}

        PAIR_TILE = P * (H // 2) * P

        counts = {e: (sem(f"{e}_steps"), CREDIT) for e in ("pe", "act", "dve", "pool")}
        stage_ended = sem("stage_ended")
        waited = {e.engine: sem(f"{name}_waited")
                  for name, e in (("dve", nc.vector), ("pe", nc.tensor), ("pool", nc.gpsimd), ("sp", nc.sync))}
        piece_in = [sem(f"piece_in{k}") for k in range(RING)]
        pieces = [0] * RING
        wo_ring = ring[:, 4 * PIECE:6 * PIECE].rearrange("p (c n) -> p c n", c=DC)
        w_out_in = {kind: sem(f"w_out_in_{kind}") for kind in ("ab", "cd")}

        block_programs = {"sp": [], "pe": [], "act": [], "dve": [], "pool": []}

        def barrier(index):
            def wait_for_all(eng):
                eng.drain().then_inc(stage_ended, 1)
                eng.wait_ge(stage_ended, 5 * index)
            return wait_for_all

        n_barriers = [0]

        def end_stage(sp, pe, act, dve, pool):
            n_barriers[0] += 1
            wait_for_all = barrier(n_barriers[0])
            for name, program in (("sp", sp), ("pe", pe), ("act", act), ("dve", dve), ("pool", pool)):
                block_programs[name] += [program, wait_for_all]

        def start():
            setup = sem("setup")

            def sp(eng):
                pass

            def pe(eng):
                eng.sem_inc(counts["pe"][0], CREDIT)

            def act(eng):
                eng.sem_inc(counts["act"][0], CREDIT)

            def dve(eng):
                eng.sem_inc(counts["dve"][0], CREDIT)
                eng.wait_ge(setup, 9)
                eng.tensor_copy(rows_to_slots[0:16, :], ident[0:16, 0:16])
                eng.tensor_copy(rows_to_slots[32:48, :], ident[32:48, 32:48])

            def pool(eng):
                eng.sem_inc(counts["pool"][0], CREDIT)
                eng.memset(ident[:, :], 0.0).then_inc(setup, 1)
                eng.memset(minus_half[:, :], -0.5).then_inc(setup, 1)
                eng.memset(rows_to_slots[:, :], 0.0).then_inc(setup, 1)
                eng.memset(gates[:, :], 0.0).then_inc(setup, 1)
                eng.memset(epsilon[:, :], EPS).then_inc(setup, 1)
                for k, width in enumerate(WIDTHS):
                    eng.memset(one_over[:, k:k + 1], 1.0 / width).then_inc(setup, 1)
                eng.wait_ge(setup, 8)
                eng.affine_select(out=ident[:, :], in_=ident[:, :], compare_op=ALU.not_equal, fill=1.0,
                                  base=0, pattern=[[-1, P]], channel_multiplier=1).then_inc(setup, 1)

            end_stage(sp, pe, act, dve, pool)

        def passed(eng):
            eng.sem_inc(waited[eng.engine], 1)

        def rsqrt_mean(eng, steps, name, n, total, mean, out, width):
            inverse = one_over[:, WIDTHS.index(width):WIDTHS.index(width) + 1]
            steps.done(name + " mean", eng.tensor_tensor(mean, total, inverse, ALU.mult))
            eng.wait_ge(steps.sem, steps.after(name + " mean", n))
            steps.done(name + " eps", eng.tensor_tensor(mean, mean, epsilon[:, :], ALU.add))
            eng.wait_ge(steps.sem, steps.after(name + " eps", n))
            steps.done(name, eng.tensor_tensor(out, mean, minus_half[:, :], ALU.pow))

        CD_PRODUCTS = ["qc", "kc", "vc", "qd", "kd", "vd"]
        cd_weights_in = [sem(f"cd_weights_in_{m}") for m in CD_PRODUCTS]
        cd_weights = [ring[:, k * PIECE:(k + 1) * PIECE].rearrange("p (c n) -> p c n", c=DC) for k in range(RING)]

        def load_cd_weights(eng, k):
            eng.dma_start(cd_weights[k], w_in_cd.rearrange("(c p) n -> p c n", p=P)[:, :, k * H * HD:(k + 1) * H * HD]
                          ).then_inc(cd_weights_in[k], 16)

        bias_spread = sem("bias_spread")

        def spread_biases(eng, pairs):
            for h in [2 * pair + e for pair in pairs for e in range(2)]:
                for r in range(2):
                    eng.dma_start(at(grid_bias, (h * P + 64 * r) * SPAN, [[GRID_W, 14], [SPAN, 64], [1, GRID_W]]),
                                  at(rpb_padded, h * 15 * P + (1 - r) * P + 63, [[P, 14], [-1, 64], [1, GRID_W]])
                                  ).then_inc(bias_spread, 16)

        def project(kind, layer, source, after):
            ab = kind == "ab"
            a = Arena()
            gain = a.take(D)
            qgain, kvgain = (a.take(QR), a.take(KVR)) if ab else (None, None)
            xt = [a.take(D) for _ in range(2)]
            ht = [a.take(D) for _ in range(2)]
            hT = [a.take(DC, P) for _ in range(2)]
            rt = [a.take(6, 64) for _ in range(2)]
            st = [a.take(16) for _ in range(2)]
            if ab:
                w_in = ring[:, 0:DC * AB_IN].rearrange("p (c n) -> p c n", c=DC)
                o = DC * AB_IN
                wuq = ring[:, o:o + 3 * H * MQ].rearrange("p (c n) -> p c n", c=3)
                o += 3 * H * MQ
                wukv = ring[:, o:o + 2 * H * 128].rearrange("p (c n) -> p c n", c=2)
                assert o + 2 * H * 128 <= 4 * PIECE
                qrow = [a.take(H, MQ) for _ in range(2)]
                krow = [a.take(H, MQ) for _ in range(2)]
                vrow = [a.take(H, MV) for _ in range(2)]
                kr = [a.take(2, ROPE) for _ in range(2)]
                mtmp = [a.take(H + 1, ROPE) for _ in range(2)]
                cqn = [a.take(3, P) for _ in range(2)]
                ckvn = [a.take(2, P) for _ in range(2)]
                cqT = [a.take(3, P) for _ in range(2)]
                ckvT = [a.take(2, P) for _ in range(2)]
                mqT = [a.take(H, P, rows=MQ) for _ in range(2)]
                mkT = [a.take(H, P, rows=MQ) for _ in range(2)]
                squares_out = [a.take(QR + KVR) for _ in range(2)]
                sq = [a.take(H, 64) for _ in range(2)]
                sq2 = [a.take(H, 64) for _ in range(2)]
                sk = [a.take(KVH, 64) for _ in range(2)]
                sk2 = [a.take(KVH, 64) for _ in range(2)]
                sv = [a.take(H, 64) for _ in range(2)]
                sqT = [a.take(4, P) for _ in range(2)]
                skT = [a.take(P) for _ in range(2)]
                columns = {"cq": (0, QR), "ckv": (QR, KVR + ROPE), "qb": (QR + KVR + ROPE, H * HD),
                           "kvb": (QR + KVR + ROPE + H * HD, 2 * KVH * HD)}
                weights_in = {m: sem(f"ab_weights_in_{m}") for m in list(columns) + ["uq", "ukv"]}
            else:
                rows = {m: [a.take(H, 64) for _ in range(2)] for m in CD_PRODUCTS}
                rows2 = {m: [a.take(H, 64) for _ in range(2)] for m in ("qc", "kc")}
                turned = {m: [a.take(4, P) for _ in range(2)] for m in ("qc", "kc", "qd", "kd")}

            gain_in = sem(f"{kind}_gain_in")
            rank_gains_in = sem("rank_gains_in") if ab else None
            x_in_s = [sem(f"{kind}_x_in{s}") for s in range(2)]
            rope_in = [sem(f"{kind}_rope_in{s}") for s in range(2)]
            rows_out = [sem(f"{kind}_rows_out{s}") for s in range(2)]
            turned_out = [sem(f"{kind}_turned_out{s}") for s in range(2)]
            N_ROWS, N_TURNED = (7, 2) if ab else (6, 0)
            ROUNDS = SEQS * T

            lags = {m: -1 for m in ("square", "x mean", "x eps", "x", "h", "h0", "h1")}
            lags.update({m: 1 for m in ("q turn0", "q turn1", "k turn0", "k turn1")})
            if ab:
                pe_names = ["cq", "ckv", "h0", "h1", "q turn0", "q turn1", "qb", "k turn0", "k turn1",
                            "cq turn", "ckv turn", "kvb", "q0", "q1", "kv0", "kv1", "sq turn", "sk turn"]
                bank_of = {"h0": 0, "k turn0": 0, "h1": 1, "k turn1": 1, "cq": 2, "q0": 2, "ckv": 3, "q1": 3,
                           "qb": 4, "kv0": 4, "kvb": 5, "kv1": 5, "q turn0": 6, "cq turn": 6, "sq turn": 6,
                           "q turn1": 7, "ckv turn": 7, "sk turn": 7}
                act_names = ["square", "cq square", "ckv square", "h0", "q turn0", "q turn1", "cq turn",
                             "q0", "q1", "sq turn"]
                dve_names = ["h", "cqn", "ckvn", "kr", "h1", "qb", "k turn0", "k turn1", "ckv turn", "sv", "kvb",
                             "kv0", "kv1", "sk turn"]
                pool_names = ["x mean", "x eps", "x", "cq mean", "cq eps", "cq", "ckv mean", "ckv eps", "ckv",
                              "kr a", "kr b", "kr sum", "sq", "sk",
                              "q rope a", "q rope b", "q rope sum"]
                emptied = {"h0": "act", "h1": "dve", "cq": ("dve", "cqn"), "ckv": ("dve", "kr"), "qb": "dve",
                           "kvb": "dve", "cq turn": "act", "ckv turn": "dve", "q0": "act", "q1": "act",
                           "kv0": "dve", "kv1": "dve", "sq turn": "act", "sk turn": "dve",
                           "q turn0": "act", "q turn1": "act", "k turn0": "dve", "k turn1": "dve"}
            else:
                turns = ["qc", "kc", "qd", "kd"]
                pe_names = ["qc", "kc", "h0", "h1", "vc", "qd", "kd", "vd"] + [m + " turn" for m in turns]
                bank_of = {"h0": 0, "h1": 1, "qc": 2, "kc": 3, "vc": 4, "qd": 5, "kd": 6, "vd": 7,
                           "qc turn": 2, "kc turn": 3, "qd turn": 5, "kd turn": 6}
                act_names = ["square", "h0", "vc", "qd", "vd", "qc turn", "qd turn"]
                dve_names = ["h", "qc", "kc", "h1", "kd", "kc turn", "kd turn"]
                pool_names = ["x mean", "x eps", "x", "qc", "kc"]
                emptied = {"h0": "act", "h1": "dve", "qc": "dve", "kc": "dve", "vc": "act", "qd": "act", "kd": "dve",
                           "vd": "act", "qc turn": "act", "qd turn": "act", "kc turn": "dve", "kd turn": "dve"}
            count = {e: len(names) for e, names in (("pe", pe_names), ("act", act_names), ("dve", dve_names), ("pool", pool_names))}
            pe_s = Steps(counts, "pe", pe_names, ROUNDS + 1, lead=count["pe"], lags=lags)
            act_s = Steps(counts, "act", act_names, ROUNDS + 1, lead=count["act"], lags=lags)
            dve_s = Steps(counts, "dve", dve_names, ROUNDS + 1, lead=count["dve"], lags=lags)
            pool_s = Steps(counts, "pool", pool_names, ROUNDS + 1, lead=count["pool"], lags=lags)
            by = {"act": act_s, "dve": dve_s}

            def rounds(eng, steps, body):
                def run(t, s, left_out):
                    steps.part(left_out)
                    body(t, s, lambda name: name not in left_out)
                lag = lambda m: lags.get(m, 0)
                run(-1, 1, [m for m in steps.names if lag(m) != -1])
                run(0, 0, [m for m in steps.names if lag(m) == 1])
                run(0, 1, [])
                with eng.Fori(1, T - 1) as t:
                    for s in range(2):
                        run(t, s, [])
                run(T - 1, 0, [])
                run(T - 1, 1, [m for m in steps.names if lag(m) == -1])
                run(T, 0, [m for m in steps.names if lag(m) != 1])
                steps.finish(eng)

            def wait_bank_empty(eng, name, n):
                b = bank_of[name]
                users = [m for m in pe_names if bank_of[m] == b]
                k = users.index(name)
                last, m = (users[k - 1], n) if k else (users[-1], n - 1)
                who = emptied[last]
                who, step = who if isinstance(who, tuple) else (who, last)
                eng.wait_ge(by[who].sem, by[who].after(step, m - lags.get(last, 0)))

            def sp(eng):
                def load_x(t, s):
                    eng.dma_start(xt[s], at(source, (t + T * s) * P * D, [[D, P], [1, D]])).then_inc(x_in_s[s], 16)

                def load_rope(t, s):
                    eng.dma_start(rt[s].rearrange("p a b -> p (a b)"),
                                  at(rope_table, t * P * 384, [[384, P], [1, 384]])).then_inc(rope_in[s], 16)

                def store_turned(t, s):
                    i = t + T * s
                    n = t * 2 + s
                    qd, kd, vd = qkv["mla"]
                    w = MQ * H * P
                    eng.wait_ge(act_s.sem, act_s.after("q turn1", n))
                    eng.dma_start(at(qd, i * w, [[H * P, MQ], [1, H * P]]),
                                  mqT[s].rearrange("p a b -> p (a b)")).then_inc(turned_out[s], 16)
                    eng.wait_ge(dve_s.sem, dve_s.after("k turn1", n))
                    eng.dma_start(at(kd, i * w, [[H * P, MQ], [1, H * P]]),
                                  mkT[s].rearrange("p a b -> p (a b)")).then_inc(turned_out[s], 16)

                def store_rows(t, s):
                    i = t + T * s
                    n = t * 2 + s
                    out = rows_out[s]
                    if ab:
                        vd = qkv["mla"][2]
                        qs, ks, vs = qkv["window"]
                        eng.wait_ge(dve_s.sem, dve_s.after("kv1", n))
                        eng.dma_start(at(vd, i * P * H * HD, [[H * HD, P], [1, H * HD]]),
                                      vrow[s].rearrange("p a b -> p (a b)")).then_inc(out, 16)
                        eng.dma_start(at(vs, i * P * H * HD, [[H * HD, P], [1, H * HD]]),
                                      sv[s].rearrange("p a b -> p (a b)")).then_inc(out, 16)
                        eng.wait_ge(dve_s.sem, dve_s.after("sk turn", n))
                        for g in range(KVH):
                            src = skT[s][64 * g:64 * g + 64, :]
                            src = src.rearrange("p (a n) -> p a n", a=1).to_broadcast([64, G // 2, P])
                            for e in range(2):
                                eng.dma_start(at(ks, i * PAIR_TILE + e * HD * 4 * P + g * (G // 2) * P,
                                                 [[4 * P, HD], [P, G // 2], [1, P]]), src).then_inc(out, 16)
                        eng.wait_ge(act_s.sem, act_s.after("sq turn", n))
                        eng.dma_start(at(qs, i * PAIR_TILE, [[4 * P, P], [1, 4 * P]]),
                                      sqT[s].rearrange("p a b -> p (a b)")).then_inc(out, 16)
                    else:
                        eng.wait_ge(act_s.sem, act_s.after("vd", n))
                        passed(eng)
                        for name, v in (("dilated", "vc"), ("grid", "vd")):
                            eng.dma_start(at(qkv[name][2], i * P * H * HD, [[H * HD, P], [1, H * HD]]),
                                          rows[v][s].rearrange("p a b -> p (a b)")).then_inc(out, 16)
                        eng.wait_ge(act_s.sem, act_s.after("qd turn", n))
                        passed(eng)
                        eng.wait_ge(dve_s.sem, dve_s.after("kd turn", n))
                        passed(eng)
                        for name, which, m in (("dilated", 0, "qc"), ("dilated", 1, "kc"),
                                               ("grid", 0, "qd"), ("grid", 1, "kd")):
                            eng.dma_start(at(qkv[name][which], i * PAIR_TILE, [[4 * P, P], [1, 4 * P]]),
                                          turned[m][s].rearrange("p a b -> p (a b)")).then_inc(out, 16)

                load_x(0, 0)
                eng.dma_start(gain, at(norm_mix, layer * D, [[0, P], [1, D]])).then_inc(gain_in, 16)
                if ab:
                    def load_columns(m):
                        first, width = columns[m]
                        eng.dma_start(w_in[:, :, first:first + width],
                                      w_in_ab.rearrange("(c p) n -> p c n", p=P)[:, :, first:first + width]
                                      ).then_inc(weights_in[m], 16)
                    load_columns("cq")
                    load_columns("ckv")
                    load_x(0, 1)
                    eng.dma_start(qgain, at(q_norm, 0, [[0, P], [1, QR]])).then_inc(rank_gains_in, 16)
                    eng.dma_start(kvgain, at(kv_norm, 0, [[0, P], [1, KVR]])).then_inc(rank_gains_in, 16)
                    load_rope(0, 0)
                    load_columns("qb")
                    load_columns("kvb")
                    eng.dma_start(wuq, w_uq.rearrange("(c p) n -> p c n", p=P)).then_inc(weights_in["uq"], 16)
                    eng.dma_start(wukv, w_ukv.rearrange("(c p) n -> p c n", p=P)).then_inc(weights_in["ukv"], 16)
                else:
                    load_rope(0, 0)
                    load_x(0, 1)
                    for k in range(4, RING):
                        load_cd_weights(eng, k)
                load_rope(0, 1)

                def body(t, s, first, last):
                    n = t * 2 + s
                    if not last:
                        eng.wait_ge(dve_s.sem, dve_s.after("h", n))
                        load_x(t + 1, s)
                    if ab and not (first and s == 0):
                        store_turned(t if s else t - 1, 1 - s)
                    if not ab and not last:
                        eng.wait_ge(dve_s.sem, dve_s.after("kc", n))
                        load_rope(t + 1, s)
                    store_rows(t, s)
                    if ab and not last:
                        eng.wait_ge(pool_s.sem, pool_s.after("q rope sum", n))
                        load_rope(t + 1, s)

                for s in range(2):
                    body(0, s, True, False)
                if not ab:
                    spread_biases(eng, (2, 3))
                with eng.Fori(1, T - 1) as t:
                    for s in range(2):
                        body(t, s, False, False)
                def all_stored(s):
                    eng.wait_ge(rows_out[s], 16 * N_ROWS * (T + 1))
                    if ab:
                        eng.wait_ge(turned_out[s], 16 * N_TURNED * (T + 1))

                body(T - 1, 0, False, True)
                if ab:
                    store_turned(T - 1, 0)
                all_stored(0)
                after.load_first(eng, 0)
                store_rows(T - 1, 1)
                if ab:
                    store_turned(T - 1, 1)
                all_stored(1)
                after.load_first(eng, 1)

            def pe(eng):
                def body(t, s, has):
                    n = t * 2 + s

                    def product(name, width, lhs, rhs_of, chunks, weights):
                        wait_bank_empty(eng, name, n)
                        eng.wait_ge(weights, 16)
                        for c in range(chunks):
                            mm = eng.matmul(bank[bank_of[name]][:, 0:width], lhs(c), rhs_of(c),
                                            start=(c == 0), stop=(c == chunks - 1))
                        pe_s.done(name, mm)

                    def turn(name, src_of, chunks, out_rows=P):
                        wait_bank_empty(eng, name, n)
                        for c in range(chunks):
                            mm = eng.transpose(bank[bank_of[name]][0:out_rows, c * P:(c + 1) * P], src_of(c), ident[:, :])
                        pe_s.done(name, mm)

                    def of_w_in(name):
                        if has(name):
                            first, width = columns[name]
                            product(name, width, lambda c: hT[s][:, c, :], lambda c: w_in[:, c, first:first + width], DC,
                                    weights_in[name])

                    def last_turns(m, row):
                        if has(m + " turn0"):
                            who, step = (pool_s, "q rope sum") if m == "q" else (dve_s, "kv1")
                            if m == "k":
                                eng.wait_ge(pool_s.sem, pool_s.after("kr sum", n - 1))
                            eng.wait_ge(who.sem, who.after(step, n - 1))
                            for k in range(2):
                                turn(f"{m} turn{k}", lambda c: row[1 - s][:, 4 * k + c, :], 4, MQ)

                    def next_h():
                        if has("h0"):
                            eng.wait_ge(dve_s.sem, dve_s.after("h", n + 1))
                            for k in range(2):
                                turn(f"h{k}", lambda c: ht[1 - s][:, (4 * k + c) * P:(4 * k + c + 1) * P], 4)

                    if has(pe_names[0]):
                        eng.wait_ge(act_s.sem, act_s.after("h0", n))
                        eng.wait_ge(dve_s.sem, dve_s.after("h1", n))
                    if ab:
                        of_w_in("cq")
                        of_w_in("ckv")
                        next_h()
                        last_turns("q", qrow)
                        of_w_in("qb")
                        last_turns("k", krow)
                        if has("cq turn"):
                            eng.wait_ge(dve_s.sem, dve_s.after("ckvn", n))
                            turn("cq turn", lambda c: cqn[s][:, c, :], 3)
                            turn("ckv turn", lambda c: ckvn[s][:, c, :], 2)
                        of_w_in("kvb")
                        if has("q0"):
                            eng.wait_ge(act_s.sem, act_s.after("cq turn", n))
                            for k in range(2):
                                product(f"q{k}", 4 * MQ, lambda c: cqT[s][:, c, :],
                                        lambda c: wuq[:, c, k * 4 * MQ:(k + 1) * 4 * MQ], 3, weights_in["uq"])
                            eng.wait_ge(dve_s.sem, dve_s.after("ckv turn", n))
                            for k in range(2):
                                product(f"kv{k}", 512, lambda c: ckvT[s][:, c, :],
                                        lambda c: wukv[:, c, k * 512:(k + 1) * 512], 2, weights_in["ukv"])
                            eng.wait_ge(pool_s.sem, pool_s.after("sk", n))
                            turn("sq turn", lambda c: sq[s].rearrange("p (c e) n -> p c (e n)", e=2)[:, c, :], 4)
                            wait_bank_empty(eng, "sk turn", n)
                            pe_s.done("sk turn", eng.transpose(
                                bank[7][:, 0:P], sk[s].rearrange("p a b -> p (a b)"), ident[:, :]))
                    else:
                        for k, m in enumerate(CD_PRODUCTS):
                            if m == "vc":
                                next_h()
                            if has(m):
                                product(m, H * HD, lambda c: hT[s][:, c, :], lambda c: cd_weights[k][:, c, :], DC,
                                        cd_weights_in[k])
                        for m in turns:
                            if has(m + " turn"):
                                who, step = {"qc": (pool_s, "qc"), "kc": (pool_s, "kc"),
                                             "qd": (act_s, "qd"), "kd": (dve_s, "kd")}[m]
                                eng.wait_ge(who.sem, who.after(step, n))
                                turn(m + " turn", lambda c: rows[m][s].rearrange("p (c e) n -> p c (e n)", e=2)[:, c, :], 4)

                rounds(eng, pe_s, body)

            def stored(eng, s, t):
                eng.wait_ge(rows_out[s], t * 16 * N_ROWS + 16 * N_ROWS)

            def stored_turned(eng, s, t):
                eng.wait_ge(turned_out[s], t * 16 * N_TURNED + 16 * N_TURNED)

            def act(eng):
                for s in range(2):
                    eng.sem_inc(rows_out[s], 16 * N_ROWS)
                    if ab:
                        eng.sem_inc(turned_out[s], 16 * N_TURNED)

                def flat(x):
                    return x.rearrange("p a b -> p (a b)")

                def body(t, s, has):
                    n = t * 2 + s

                    def copy(name, out, width=BANK, rows=P, tile=n, **scale):
                        if has(name):
                            eng.wait_ge(pe_s.sem, pe_s.after(name, tile))
                            act_s.done(name, eng.activation(out, bank[bank_of[name]][0:rows, 0:width], ACT.Copy, **scale))

                    def square(name, out, src, total):
                        act_s.done(name, eng.activation(out, src, ACT.Square, accum_out=total))

                    if has("square"):
                        eng.wait_ge(x_in_s[1 - s], (t if s == 0 else t + 1) * 16 + 16)
                        eng.wait_ge(pe_s.sem, pe_s.after("h1", n - 1))
                        square("square", ht[1 - s], xt[1 - s], st[1 - s][:, 0:1])
                    if ab:
                        if has("cq square"):
                            eng.wait_ge(pe_s.sem, pe_s.after("cq", n))
                            square("cq square", squares_out[s][:, 0:QR], bank[2][:, 0:QR], st[s][:, 3:4])
                            eng.wait_ge(pe_s.sem, pe_s.after("ckv", n))
                            square("ckv square", squares_out[s][:, QR:], bank[3][:, 0:KVR], st[s][:, 6:7])
                        copy("h0", flat(hT[1 - s])[:, 0:512], tile=n + 1)
                        if has("q turn0"):
                            stored_turned(eng, 1 - s, t if s else t - 1)
                        for k in range(2):
                            copy(f"q turn{k}", flat(mqT[1 - s][:, 4 * k:4 * k + 4, :]), rows=MQ, tile=n - 1)
                        copy("cq turn", flat(cqT[s]), QR)
                        for k in range(2):
                            copy(f"q{k}", flat(qrow[s][:, 4 * k:4 * k + 4, :]), 4 * MQ, scale=float(MQ) ** -0.5)
                        if has("sq turn"):
                            stored(eng, s, t)
                        copy("sq turn", flat(sqT[s]))
                    else:
                        copy("h0", flat(hT[1 - s])[:, 0:512], tile=n + 1)
                        if has("vc"):
                            stored(eng, s, t)
                        for m, scale in (("vc", 1.0), ("qd", HD ** -0.5), ("vd", 1.0)):
                            copy(m, flat(rows[m][s]), scale=scale)
                        for m in ("qc", "qd"):
                            copy(m + " turn", flat(turned[m][s]))

                rounds(eng, act_s, body)

            def per_head(table, k, heads):
                return table[:, k:k + 1, :].to_broadcast([P, heads, 64])

            def dve(eng):
                def rope_products(out, out2, src, table, k, heads):
                    eng.tensor_tensor(out, src, per_head(table, k, heads), ALU.mult)
                    eng.tensor_tensor(out2[:, :, 0:32], src[:, :, 32:64], per_head(table, k + 1, heads)[:, :, 0:32], ALU.mult)
                    return eng.tensor_tensor(out2[:, :, 32:64], src[:, :, 0:32],
                                             per_head(table, k + 1, heads)[:, :, 32:64], ALU.mult)

                def flat(x):
                    return x.rearrange("p a b -> p (a b)")

                def body(t, s, has):
                    n = t * 2 + s

                    def copy(name, out, width=BANK, rows=P, tile=n):
                        if has(name):
                            eng.wait_ge(pe_s.sem, pe_s.after(name, tile))
                            dve_s.done(name, eng.tensor_copy(out, bank[bank_of[name]][0:rows, 0:width]))

                    def scaled(name, out, src, scale, by_gain):
                        dve_s.done(name, eng.scalar_tensor_tensor(out=out, in0=src, scalar=scale, in1=by_gain,
                                                                  op0=ALU.mult, op1=ALU.mult))

                    if has("h"):
                        eng.wait_ge(pool_s.sem, pool_s.after("x", n + 1))
                        scaled("h", ht[1 - s], xt[1 - s], st[1 - s][:, 2:3], gain)
                    if ab:
                        if has("cqn"):
                            eng.wait_ge(rank_gains_in, 32)
                            eng.wait_ge(pool_s.sem, pool_s.after("cq", n))
                            scaled("cqn", flat(cqn[s]), bank[2][:, 0:QR], st[s][:, 5:6], qgain)
                            eng.wait_ge(pool_s.sem, pool_s.after("ckv", n))
                            scaled("ckvn", flat(ckvn[s]), bank[3][:, 0:KVR], st[s][:, 8:9], kvgain)
                            dve_s.done("kr", eng.tensor_copy(kr[s][:, 0, :], bank[3][:, KVR:KVR + ROPE]))
                        copy("h1", flat(hT[1 - s])[:, 512:1024], tile=n + 1)
                        if has("qb"):
                            eng.wait_ge(rope_in[s], t * 16 + 16)
                            eng.wait_ge(pe_s.sem, pe_s.after("qb", n))
                            dve_s.done("qb", rope_products(sq[s], sq2[s], bank[4][:, :].rearrange("p (h d) -> p h d", h=H),
                                                           rt[s], 0, H))
                        if has("k turn0"):
                            stored_turned(eng, 1 - s, t if s else t - 1)
                        for k in range(2):
                            copy(f"k turn{k}", flat(mkT[1 - s][:, 4 * k:4 * k + 4, :]), rows=MQ, tile=n - 1)
                        copy("ckv turn", flat(ckvT[s]), KVR)
                        if has("kvb"):
                            stored(eng, s, t)
                            eng.wait_ge(pe_s.sem, pe_s.after("kvb", n))
                            v = bank[5][:, KVH * HD:2 * KVH * HD]
                            for g in range(KVH):
                                ins = eng.tensor_copy(
                                    sv[s][:, G * g:G * g + G, :],
                                    v[:, g * HD:(g + 1) * HD].rearrange("p (a d) -> p a d", a=1).to_broadcast([P, G, HD]))
                            dve_s.done("sv", ins)
                            dve_s.done("kvb", rope_products(
                                sk[s], sk2[s], bank[5][:, 0:KVH * HD].rearrange("p (h d) -> p h d", h=KVH), rt[s], 2, KVH))
                            for k in range(2):
                                eng.wait_ge(pe_s.sem, pe_s.after(f"kv{k}", n))
                                kv = bank[4 + k][:, :].rearrange("p (h d) -> p h d", h=4)
                                eng.tensor_copy(krow[s][:, 4 * k:4 * k + 4, 0:NOPE], kv[:, :, 0:NOPE])
                                dve_s.done(f"kv{k}", eng.tensor_copy(vrow[s][:, 4 * k:4 * k + 4, :], kv[:, :, NOPE:NOPE + MV]))
                        copy("sk turn", skT[s], P)
                    else:
                        if has("qc"):
                            eng.wait_ge(rope_in[s], t * 16 + 16)
                            stored(eng, s, t)
                        for m, k in (("qc", 0), ("kc", 2)):
                            if has(m):
                                eng.wait_ge(pe_s.sem, pe_s.after(m, n))
                                dve_s.done(m, rope_products(rows[m][s], rows2[m][s],
                                                            bank[bank_of[m]][:, :].rearrange("p (h d) -> p h d", h=H),
                                                            rt[s], k, H))
                        copy("h1", flat(hT[1 - s])[:, 512:1024], tile=n + 1)
                        copy("kd", flat(rows["kd"][s]))
                        for m in ("kc", "kd"):
                            copy(m + " turn", flat(turned[m][s]))

                eng.wait_ge(gain_in, 16)
                rounds(eng, dve_s, body)

            def pool(eng):
                def cos(table, k, heads):
                    return table[:, k:k + 1, 0:32].to_broadcast([P, heads, 32])

                def sin(table, k, heads):
                    return table[:, k:k + 1, 32:64].to_broadcast([P, heads, 32])

                def rope32(name, n, src, product, tmp, tmp_rows, table, k, heads, out):
                    lo, hi = slice(0, 16), slice(16, 32)
                    eng.tensor_tensor(tmp[:, tmp_rows, lo], src[:, :, hi], sin(table, k, heads)[:, :, lo], ALU.mult)
                    pool_s.done(name + " a", eng.tensor_tensor(tmp[:, tmp_rows, hi], src[:, :, lo],
                                                               sin(table, k, heads)[:, :, hi], ALU.mult))
                    eng.wait_ge(pool_s.sem, pool_s.after(name + " a", n))
                    pool_s.done(name + " b", eng.tensor_tensor(product, src, cos(table, k, heads), ALU.mult))
                    eng.wait_ge(pool_s.sem, pool_s.after(name + " b", n))
                    pool_s.done(name + " sum", eng.tensor_tensor(
                        out, product.to_broadcast(list(out.shape)), tmp[:, tmp_rows, :].to_broadcast(list(out.shape)), ALU.add))

                def body(t, s, has):
                    n = t * 2 + s
                    if has("x"):
                        o = st[1 - s]
                        eng.wait_ge(act_s.sem, act_s.after("square", n + 1))
                        rsqrt_mean(eng, pool_s, "x", n + 1, o[:, 0:1], o[:, 1:2], o[:, 2:3], D)
                    if ab and has("cq"):
                        eng.wait_ge(act_s.sem, act_s.after("cq square", n))
                        rsqrt_mean(eng, pool_s, "cq", n, st[s][:, 3:4], st[s][:, 4:5], st[s][:, 5:6], QR)
                        eng.wait_ge(act_s.sem, act_s.after("ckv square", n))
                        rsqrt_mean(eng, pool_s, "ckv", n, st[s][:, 6:7], st[s][:, 7:8], st[s][:, 8:9], KVR)
                        eng.wait_ge(dve_s.sem, dve_s.after("kr", n))
                        eng.wait_ge(rope_in[s], t * 16 + 16)
                        eng.wait_ge(pe_s.sem, pe_s.after("k turn1", n - 2))
                        rope32("kr", n, kr[s][:, 0:1, :], kr[s][:, 1:2, :], mtmp[s], slice(H, H + 1), rt[s], 5, 1,
                               krow[s][:, :, NOPE:MQ])
                        eng.wait_ge(dve_s.sem, dve_s.after("qb", n))
                        pool_s.done("sq", eng.tensor_tensor(sq[s], sq[s], sq2[s], ALU.add))
                        eng.wait_ge(dve_s.sem, dve_s.after("kvb", n))
                        pool_s.done("sk", eng.tensor_tensor(sk[s], sk[s], sk2[s], ALU.add))
                        eng.wait_ge(act_s.sem, act_s.after("q1", n))
                        rope32("q rope", n, qrow[s][:, :, NOPE:MQ], qrow[s][:, :, NOPE:MQ], mtmp[s], slice(0, H), rt[s], 5, H,
                               qrow[s][:, :, NOPE:MQ])
                    elif not ab and has("qc"):
                        for m in ("qc", "kc"):
                            eng.wait_ge(dve_s.sem, dve_s.after(m, n))
                            pool_s.done(m, eng.tensor_tensor(rows[m][s], rows[m][s], rows2[m][s], ALU.add))

                if after.biased:
                    after.zero(eng)
                rounds(eng, pool_s, body)

            end_stage(sp, pe, act, dve, pool)

        class AttentionInputs:

            def __init__(self, kind, start, memory=None, end=ARENA):
                self.kind, self.biased = kind, kind != "mla"
                a = Arena(start, memory, end)
                width = P if self.biased else MQ
                self.q, self.k, self.v = [], [], []
                for _ in range(2):
                    self.q.append(a.take(T, 2, P, rows=width))
                    self.k.append(a.take(T, 1 if self.biased else 2, P, rows=width))
                    self.v.append(a.take(T, 2 * HD))
                self.sinks = a.take(2, 2) if kind == "window" else None
                self.table = a.take(1, SPAN) if kind in ("window", "dilated") else None
                self.raw, self.column_mask = (a.take(2, SPAN), a.take(GRID_W)) if kind == "grid" else (None, None)
                self.qkv_in = [sem(f"{kind}_qkv_in{s}") for s in range(2)]
                self.loads = {"mla": 3, "window": 5, "dilated": 4, "grid": 4}[kind]
                self.table_in = sem(f"{kind}_table_in")
                self.q_zeroed = [sem(f"{kind}_q_zeroed{s}") for s in range(2)]

            def zero(self, eng):
                for s in range(2):
                    eng.memset(self.q[s], 0.0).then_inc(self.q_zeroed[s], 1)

            def load(self, eng, pair, s):
                qd, kd, vd = qkv[self.kind]
                q, k, v, qkv_in = self.q, self.k, self.v, self.qkv_in
                if self.biased:
                    eng.dma_start(k[s][:, :, 0, :], at(kd, pair * P + T * s * PAIR_TILE,
                                                       [[4 * P, P], [PAIR_TILE, T], [1, P]])).then_inc(qkv_in[s], 16)
                    for e in range(2):
                        eng.dma_start(q[s][64 * e:64 * e + 64, :, e, :],
                                      at(qd, pair * P + T * s * PAIR_TILE + e * HD * 4 * P,
                                         [[4 * P, HD], [PAIR_TILE, T], [1, P]])).then_inc(qkv_in[s], 16)
                else:
                    w = MQ * H * P
                    for dst, src in ((q, qd), (k, kd)):
                        eng.dma_start(dst[s].rearrange("p t e n -> p t (e n)"),
                                      at(src, pair * (2 * P) + T * s * w, [[H * P, MQ], [w, T], [1, 2 * P]])
                                      ).then_inc(qkv_in[s], 16)
                eng.dma_start(v[s], at(vd, pair * (2 * HD) + T * s * P * H * HD,
                                       [[H * HD, P], [P * H * HD, T], [1, 2 * HD]])).then_inc(qkv_in[s], 16)
                if self.kind == "window":
                    eng.dma_start(self.sinks[:, s, :], at(sink, pair * 2, [[0, P], [1, 2]])).then_inc(qkv_in[s], 16)

            def load_bias(self, eng, pair):
                eng.dma_start(self.raw, at(grid_bias, pair * (2 * P * SPAN), [[SPAN, P], [P * SPAN, 2], [1, SPAN]])
                              ).then_inc(self.table_in, 16)

            def load_first(self, eng, s):
                if self.biased:
                    eng.wait_ge(self.q_zeroed[s], 1)
                self.load(eng, 0, s)
                if s == 0 and self.kind in ("window", "dilated"):
                    eng.dma_start(self.table[:, 0, :], window_table if self.kind == "window" else dilated_table
                                  ).then_inc(self.table_in, 16)
                if s == 0 and self.kind == "grid":
                    eng.dma_start(self.column_mask, column_table).then_inc(self.table_in, 16)
                    eng.wait_ge(bias_spread, 16 * 2 * H)
                    self.load_bias(eng, 0)

        def attention(inputs, column, start, prefetch=None, zero_next=None, next_early=None, next_late=None):
            kind, biased = inputs.kind, inputs.biased
            q, k, v, qkv_in, table_in = inputs.q, inputs.k, inputs.v, inputs.qkv_in, inputs.table_in
            a = Arena(start)
            o = [a.take(T, 2 * HD) for _ in range(2)]
            p = [a.take(T, P) for _ in range(4)]
            pT = [a.take(T, P) for _ in range(2)]
            masked = [a.take(T, P) for _ in range(4)] if biased else None
            stat = a.take(4, 16)
            sinks, raw, column_mask = inputs.sinks, inputs.raw, inputs.column_mask
            table = a.take(2, SPAN) if kind == "grid" else inputs.table
            U = 16
            LAG = 2
            PAIRS = H // 2
            units = [(s, hh, t) for s in range(2) for hh in range(2) for t in range(T)]

            o_out = [sem(f"{kind}_o_out{s}") for s in range(2)]

            def blocks(t):
                return (max(0, t - 1), min(T, t + 2)) if kind == "window" else (0, T)

            def piped(pieces):
                for i in range(U + LAG + 1):
                    for piece, lag in pieces:
                        if 0 <= i - lag < U:
                            yield piece, i - lag

            PE_PIECES = [("qk", 0), ("turn", LAG), ("pv", LAG + 1)]
            ACT_PIECES = [("turn", LAG), ("exp", 0)]
            DVE_PIECES = [("turn", LAG), ("max", 0), ("recip", LAG), ("out", LAG + 1)]

            pe_s = Steps(counts, "pe", [f"{w}{u}" for w, u in piped(PE_PIECES)], PAIRS)
            act_names = []
            for w, u in piped(ACT_PIECES):
                if w == "exp":
                    act_names.append(f"exp{u}")
                    if kind == "window":
                        act_names.append(f"sink{u}")
                elif u % 2:
                    act_names.append(f"turn{u}")
            act_s = Steps(counts, "act", act_names, PAIRS)
            dve_names = []
            for w, u in piped(DVE_PIECES):
                if w == "recip" and kind == "window":
                    dve_names.append(f"sum{u}")
                if w != "turn" or not u % 2:
                    dve_names.append(f"{w}{u}")
            dve_s = Steps(counts, "dve", dve_names, PAIRS)
            pool_s = Steps(counts, "pool", ["table"], PAIRS) if kind == "grid" else None

            def earlier(u, pair, back):
                return ((u - back) % U, pair if u >= back else pair - 1)

            def wait_unit(eng, steps, step, u, pair, back):
                m, r = earlier(u, pair, back)
                eng.wait_ge(steps.sem, steps.after(f"{step}{m}", r))

            def turner(u):
                return act_s if u % 2 else dve_s

            def sp(eng):
                if prefetch:
                    prefetch(eng)

                def store(pair, s):
                    eng.wait_ge(dve_s.sem, dve_s.after(f"out{8 * s + 7}", pair))
                    eng.dma_start(at(mixed, pair * (2 * HD) + T * s * P * D + column, [[D, P], [P * D, T], [1, 2 * HD]]),
                                  o[s]).then_inc(o_out[s], 16)

                with eng.Fori(0, PAIRS - 1) as pair:
                    if kind == "grid":
                        eng.wait_ge(pool_s.sem, pool_s.after("table", pair))
                        inputs.load_bias(eng, pair + 1)
                    for s in range(2):
                        store(pair, s)
                        inputs.load(eng, pair + 1, s)
                if next_early:
                    next_early(eng)
                store(PAIRS - 1, 0)
                eng.wait_ge(o_out[0], 16 * (PAIRS + 1))
                if next_late:
                    next_late(eng)
                store(PAIRS - 1, 1)
                eng.wait_ge(o_out[1], 16 * (PAIRS + 1))

            def pe(eng):
                with eng.Fori(0, PAIRS) as pair:
                    for w, u in piped(PE_PIECES):
                        s, e, t = units[u]
                        b0, b1 = blocks(t)
                        if w == "qk":
                            if u % 8 == 0:
                                n = 16 * inputs.loads
                                eng.wait_ge(qkv_in[s], pair * n + n)
                            wait_unit(eng, dve_s if biased else act_s, "max" if biased else "exp", u, pair, 4)
                            pe_s.done(f"qk{u}", eng.matmul(
                                bank[u % 4][:, 0:(b1 - b0) * P].rearrange("p (b n) -> p b n", n=P), q[s][:, t, e, :],
                                k[s][:, b0:b1, 0 if biased else e, :], start=True, stop=True))
                        elif w == "turn":
                            wait_unit(eng, act_s, "exp", u, pair, 0)
                            wait_unit(eng, turner(u), "turn", u, pair, 2)
                            for b in range(b1 - b0):
                                mm = eng.transpose(bank[4 + u % 2][:, b * P:(b + 1) * P], p[u % 4][:, b, :], ident[:, :])
                            pe_s.done(f"turn{u}", mm)
                        else:
                            wait_unit(eng, turner(u), "turn", u, pair, 0)
                            wait_unit(eng, dve_s, "out", u, pair, 2)
                            for b in range(b1 - b0):
                                mm = eng.matmul(bank[6 + u % 2][:, 0:HD], pT[u % 2][:, b, :],
                                                v[s][:, b0 + b, e * HD:(e + 1) * HD], start=(b == 0), stop=(b == b1 - b0 - 1))
                            pe_s.done(f"pv{u}", mm)

            def flat(tile, n):
                return tile.rearrange("p a b -> p (a b)")[:, 0:n]

            def act(eng):
                for s in range(2):
                    eng.sem_inc(o_out[s], 16)
                with eng.Fori(0, PAIRS) as pair:
                    for w, u in piped(ACT_PIECES):
                        s, e, t = units[u]
                        b0, b1 = blocks(t)
                        n = (b1 - b0) * P
                        if w == "exp":
                            wait_unit(eng, dve_s, "max", u, pair, 0)
                            wait_unit(eng, pe_s, "turn", u, pair, 4)
                            src = flat(masked[u % 4], n) if biased else bank[u % 4][:, 0:n]
                            act_s.done(f"exp{u}", eng.activation(
                                flat(p[u % 4], n), src, ACT.Exp, bias=stat[:, 0, u:u + 1],
                                scale=-1.0 if biased else 1.0, accum_out=stat[:, 1, u:u + 1]))
                            if kind == "window":
                                act_s.done(f"sink{u}", eng.activation(stat[:, 2, u:u + 1], stat[:, 0, u:u + 1], ACT.Exp,
                                                                      bias=sinks[:, s, e:e + 1], scale=1.0))
                        elif u % 2:
                            wait_unit(eng, pe_s, "turn", u, pair, 0)
                            wait_unit(eng, pe_s, "pv", u, pair, 2)
                            act_s.done(f"turn{u}", eng.activation(flat(pT[u % 2], n), bank[4 + u % 2][:, 0:n], ACT.Copy))

            def dve(eng):
                if biased and kind != "grid":
                    eng.wait_ge(table_in, 16)
                with eng.Fori(0, PAIRS) as pair:
                    if kind == "grid":
                        eng.wait_ge(pool_s.sem, pool_s.after("table", pair))
                    for w, u in piped(DVE_PIECES):
                        s, e, t = units[u]
                        b0, b1 = blocks(t)
                        n = (b1 - b0) * P
                        if w == "max":
                            wait_unit(eng, pe_s, "qk", u, pair, 0)
                            if biased:
                                wait_unit(eng, act_s, "exp", u, pair, 4)
                                c = SEQ - P - P * t + P * b0
                                bias = table[:, e if kind == "grid" else 0, c:c + n]
                                passed(eng)
                                dve_s.done(f"max{u}", eng.tensor_tensor_reduce(
                                    flat(masked[u % 4], n), bank[u % 4][:, 0:n], bias, -1.0, BIG, ALU.add, ALU.min,
                                    stat[:, 0, u:u + 1]))
                            else:
                                dve_s.done(f"max{u}", eng.tensor_reduce(stat[:, 0, u:u + 1], bank[u % 4][:, 0:n], AX.X,
                                                                        ALU.max, negate=True))
                        elif w == "turn":
                            if not u % 2:
                                wait_unit(eng, pe_s, "turn", u, pair, 0)
                                wait_unit(eng, pe_s, "pv", u, pair, 2)
                                dve_s.done(f"turn{u}", eng.tensor_copy(flat(pT[u % 2], n), bank[4 + u % 2][:, 0:n]))
                        elif w == "recip":
                            if kind == "window":
                                wait_unit(eng, act_s, "sink", u, pair, 0)
                                dve_s.done(f"sum{u}", eng.tensor_tensor(stat[:, 1, u:u + 1], stat[:, 1, u:u + 1],
                                                                        stat[:, 2, u:u + 1], ALU.add))
                                wait_unit(eng, dve_s, "sum", u, pair, 0)
                            else:
                                wait_unit(eng, act_s, "exp", u, pair, 0)
                            dve_s.done(f"recip{u}", eng.reciprocal(stat[:, 3, u:u + 1], stat[:, 1, u:u + 1]))
                        else:
                            if u % 8 == 0:
                                eng.wait_ge(o_out[s], pair * 16 + 16)
                            wait_unit(eng, pe_s, "pv", u, pair, 0)
                            wait_unit(eng, dve_s, "recip", u, pair, 0)
                            dve_s.done(f"out{u}", eng.tensor_scalar(o[s][:, t, e * HD:(e + 1) * HD], bank[6 + u % 2][:, 0:HD],
                                                                    stat[:, 3, u:u + 1], None, ALU.mult))

            def pool(eng):
                if zero_next:
                    zero_next(eng)
                if kind != "grid":
                    return
                with eng.Fori(0, PAIRS) as pair:
                    eng.wait_ge(table_in, pair * 16 + 32)
                    wait_unit(eng, dve_s, "max", U - 1, pair - 1, 0)
                    pool_s.done("table", eng.tensor_tensor(
                        table.rearrange("p e (a b) -> p (e a) b", b=GRID_W), raw.rearrange("p e (a b) -> p (e a) b", b=GRID_W),
                        column_mask.rearrange("p (a b) -> p a b", a=1).to_broadcast([P, 28, GRID_W]), ALU.add))

            end_stage(sp, pe, act, dve, pool)

        def load_w_out(kind, w_out):
            def prefetch(eng):
                eng.dma_start(wo_ring, w_out.rearrange("(c p) n -> p c n", p=P)).then_inc(w_out_in[kind], 16)
            return prefetch

        class OutputInputs:

            def __init__(self, kind, layer, source):
                self.kind, self.layer, self.source = kind, layer, source
                a = Arena()
                self.ot = [a.take(D) for _ in range(2)]
                self.xt = [a.take(D) for _ in range(2)]
                self.gain = a.take(D)
                self.router = a.take(DC, E)
                self.rest = a.at
                self.const_in = sem(f"{kind}o_const_in")
                self.rows_in = [sem(f"{kind}o_rows_in{s}") for s in range(2)]
                self.x_in = [sem(f"{kind}o_x_in{s}") for s in range(2)]

            def load_early(self, eng):
                eng.dma_start(self.router, at(w_router, self.layer * D * E, [[E, P], [P * E, DC], [1, E]])
                              ).then_inc(self.const_in, 16)
                eng.dma_start(self.gain, at(norm_ffn, self.layer * D, [[0, P], [1, D]])).then_inc(self.const_in, 16)
                for s in range(2):
                    eng.dma_start(self.xt[s], at(self.source, T * s * P * D, [[D, P], [1, D]])).then_inc(self.x_in[s], 16)

            def load_rows(self, eng, s):
                eng.dma_start(self.ot[s], at(mixed, T * s * P * D, [[D, P], [1, D]])).then_inc(self.rows_in[s], 16)

        def output(inputs):
            kind, source = inputs.kind, inputs.source
            ot, xt, gain, router = inputs.ot, inputs.xt, inputs.gain, inputs.router
            const_in, rows_in, x_in_s = inputs.const_in, inputs.rows_in, inputs.x_in
            a = Arena(inputs.rest)
            oT = [a.take(DC, P) for _ in range(2)]
            xn = [a.take(D) for _ in range(2)]
            squares_out = a.take(D)
            h = [a.take(D) for _ in range(2)]
            hT = [a.take(DC, P) for _ in range(2)]
            logits = [a.take(E) for _ in range(2)]
            aff = a.take(48)
            st = [a.take(16) for _ in range(2)]

            x_out = [sem(f"{kind}o_x_out{s}") for s in range(2)]
            aff_zero = sem(f"{kind}o_aff_zero")

            pe_names = ["ya0", "oT0 1", "oT1 1", "hT0 1", "hT1 1", "yb0", "r1",
                        "ya1", "oT0 0", "oT1 0", "hT0 0", "hT1 0", "aff", "yb1", "r0"]
            lags = {"oT0 0": -1, "oT1 0": -1, "oT 0": -1, "hT0 1": 1, "hT1 1": 1, "hT 1": 1, "r1": 1, "aff": 1,
                    "exp1": 1, "rmax1": 1, "recip1": 1, "aff1": 1}
            pe_s = Steps(counts, "pe", pe_names, T + 1, lead=7, lags=lags)
            act_s = Steps(counts, "act", ["oT 1", "hT 1", "square0", "exp1", "oT 0", "hT 0", "square1", "exp0"], T + 1,
                          lead=4, lags=lags)
            dve_s = Steps(counts, "dve", ["adda0", "oT 1", "hT 1", "addb0", "rmax1", "h0", "recip1", "aff1",
                                          "adda1", "oT 0", "hT 0", "aff", "addb1", "rmax0", "h1", "recip0", "aff0"], T + 1,
                          lead=8, lags=lags)
            pool_s = Steps(counts, "pool", [f"x{s}{m}" for s in range(2) for m in (" mean", " eps", "")], T)

            def parts(eng, steps, body):
                first = [m for m in steps.names if lags.get(m) == 1]
                last = [m for m in steps.names if lags.get(m) == -1]
                tail = [m for m in steps.names if lags.get(m) != 1]
                steps.part(first)
                body(0, first)
                steps.part()
                with eng.Fori(1, T - 1) as t:
                    body(t, ())
                steps.part(last)
                body(T - 1, last)
                steps.part(tail)
                body(T, tail)

            def sp(eng):
                tile = [[D, P], [1, D]]
                inputs.load_rows(eng, 1)
                load_piece(eng, inputs.layer, 0, 0)
                load_piece(eng, inputs.layer, 0, 1)

                def store_x(t, s):
                    eng.wait_ge(dve_s.sem, dve_s.after(f"addb{s}", t))
                    eng.dma_start(at(residual, (t + T * s) * P * D, tile), xn[s]).then_inc(x_out[s], 16)

                def load(t, s):
                    eng.dma_start(ot[s], at(mixed, (t + T * s) * P * D, tile)).then_inc(rows_in[s], 16)
                    eng.dma_start(xt[s], at(source, (t + T * s) * P * D, tile)).then_inc(x_in_s[s], 16)

                def store_h(t, s):
                    eng.wait_ge(dve_s.sem, dve_s.after(f"h{s}", t))
                    eng.dma_start(at(normed, (t + T * s) * P * D, tile), h[s]).then_inc(x_out[s], 16)

                with eng.Fori(0, T - 1) as t:
                    for s in range(2):
                        store_x(t, s)
                        load(t + 1, s)
                        store_h(t, s)
                store_x(T - 1, 0)
                store_h(T - 1, 0)
                store_x(T - 1, 1)
                store_h(T - 1, 1)
                load_piece(eng, inputs.layer, 0, 2)
                load_piece(eng, inputs.layer, 0, 3)
                for s in range(2):
                    eng.wait_ge(x_out[s], 32 * (T + 1))

            def pe(eng):
                def turn_rows(t, s, done):
                    eng.wait_ge(rows_in[s], t * 16 + 16)
                    for k in range(2):
                        who = act_s if k == 0 else dve_s
                        eng.wait_ge(who.sem, who.after(f"oT {1 - s}", t if s else t - 1))
                        for c in range(4):
                            mm = eng.transpose(bank[k][:, c * P:(c + 1) * P],
                                               ot[s][:, (4 * k + c) * P:(4 * k + c + 1) * P], ident[:, :])
                        done(k, mm)

                def body(t, left_out):
                    for s in range(2):
                        before = t if s else t - 1

                        def half(k, name):
                            if name in left_out:
                                return
                            eng.wait_ge(dve_s.sem, dve_s.after(f"add{'ab'[k]}{1 - s}", before))
                            for c in range(DC):
                                mm = eng.matmul(bank[2 + k][:, :], oT[s][:, c, :], wo_ring[:, c, k * BANK:(k + 1) * BANK],
                                                start=(c == 0), stop=(c == DC - 1))
                            pe_s.done(name, mm)

                        if f"ya{s}" not in left_out:
                            eng.wait_ge(act_s.sem, act_s.after(f"oT {s}", t))
                            eng.wait_ge(dve_s.sem, dve_s.after(f"oT {s}", t))
                        half(0, f"ya{s}")
                        if f"oT0 {1 - s}" not in left_out:
                            turn_rows(t if s == 0 else t + 1, 1 - s, lambda k, mm: pe_s.done(f"oT{k} {1 - s}", mm))
                        if f"hT0 {1 - s}" not in left_out:
                            eng.wait_ge(dve_s.sem, dve_s.after(f"h{1 - s}", before))
                            for k in range(2):
                                who = act_s if k == 0 else dve_s
                                eng.wait_ge(who.sem, who.after(f"hT {s}", t - 1))
                                for c in range(4):
                                    mm = eng.transpose(bank[4 + k][:, c * P:(c + 1) * P],
                                                       h[1 - s][:, (4 * k + c) * P:(4 * k + c + 1) * P], ident[:, :])
                                pe_s.done(f"hT{k} {1 - s}", mm)
                        if s and "aff" not in left_out:
                            eng.wait_ge(dve_s.sem, dve_s.after("aff1", t - 1))
                            passed(eng)
                            pe_s.done("aff", eng.transpose(bank[7][0:48, 0:P], aff, ident[:, :]))
                        half(1, f"yb{s}")
                        if f"r{1 - s}" not in left_out:
                            eng.wait_ge(act_s.sem, act_s.after(f"hT {1 - s}", before))
                            eng.wait_ge(dve_s.sem, dve_s.after(f"hT {1 - s}", before))
                            eng.wait_ge(act_s.sem, act_s.after(f"exp{s}", t - 1))
                            for c in range(DC):
                                mm = eng.matmul(bank[6][:, 0:E], hT[1 - s][:, c, :], router[:, c, :],
                                                start=(c == 0), stop=(c == DC - 1))
                            pe_s.done(f"r{1 - s}", mm)

                eng.wait_ge(rows_in[0], 16)
                for k in range(2):
                    for c in range(4):
                        mm = eng.transpose(bank[k][:, c * P:(c + 1) * P],
                                           ot[0][:, (4 * k + c) * P:(4 * k + c + 1) * P], ident[:, :])
                    mm.then_inc(pe_s.sem, 6 if k else 1)
                eng.wait_ge(const_in, 32)
                eng.wait_ge(w_out_in[kind], 16)
                parts(eng, pe_s, body)

            def act(eng):
                def take_rows(s):
                    return eng.activation(oT[s].rearrange("p a b -> p (a b)")[:, 0:512], bank[0][:, :], ACT.Copy)

                def body(t, left_out):
                    for s in range(2):
                        before = t if s else t - 1
                        if f"oT {1 - s}" not in left_out:
                            eng.wait_ge(pe_s.sem, pe_s.after(f"oT0 {1 - s}", t if s == 0 else t + 1))
                            act_s.done(f"oT {1 - s}", take_rows(1 - s))
                        if f"hT {1 - s}" not in left_out:
                            eng.wait_ge(pe_s.sem, pe_s.after(f"hT0 {1 - s}", before))
                            act_s.done(f"hT {1 - s}", eng.activation(
                                hT[1 - s].rearrange("p a b -> p (a b)")[:, 0:512], bank[4][:, :], ACT.Copy))
                        if f"square{s}" not in left_out:
                            eng.wait_ge(dve_s.sem, dve_s.after(f"addb{s}", t))
                            act_s.done(f"square{s}", eng.activation(squares_out, xn[s], ACT.Square, accum_out=st[s][:, 0:1]))
                        if f"exp{1 - s}" not in left_out:
                            eng.wait_ge(dve_s.sem, dve_s.after(f"rmax{1 - s}", before))
                            act_s.done(f"exp{1 - s}", eng.activation(
                                logits[1 - s], bank[6][:, 0:E], ACT.Exp, bias=st[1 - s][:, 3:4], scale=1.0,
                                accum_out=st[1 - s][:, 4:5]))

                for s in range(2):
                    eng.sem_inc(x_out[s], 32)
                eng.wait_ge(pe_s.sem, pe_s.after("oT0 0", 0))
                take_rows(0).then_inc(act_s.sem, 4)
                parts(eng, act_s, body)

            def dve(eng):
                def take_rows(s):
                    return eng.tensor_copy(oT[s].rearrange("p a b -> p (a b)")[:, 512:1024], bank[1][:, :])

                def body(t, left_out):
                    for s in range(2):
                        before = t if s else t - 1

                        def add(k, name):
                            if name in left_out:
                                return
                            half = slice(k * BANK, (k + 1) * BANK)
                            eng.wait_ge(pe_s.sem, pe_s.after(f"y{'ab'[k]}{s}", t))
                            dve_s.done(name, eng.tensor_tensor(xn[s][:, half], bank[2 + k][:, :], xt[s][:, half], ALU.add))

                        if f"adda{s}" not in left_out:
                            eng.wait_ge(x_out[s], t * 32 + 32)
                            eng.wait_ge(x_in_s[s], t * 16 + 16)
                        add(0, f"adda{s}")
                        if f"oT {1 - s}" not in left_out:
                            eng.wait_ge(pe_s.sem, pe_s.after(f"oT1 {1 - s}", t if s == 0 else t + 1))
                            dve_s.done(f"oT {1 - s}", take_rows(1 - s))
                        if f"hT {1 - s}" not in left_out:
                            eng.wait_ge(pe_s.sem, pe_s.after(f"hT1 {1 - s}", before))
                            dve_s.done(f"hT {1 - s}", eng.tensor_copy(
                                hT[1 - s].rearrange("p a b -> p (a b)")[:, 512:1024], bank[5][:, :]))
                        if s and "aff" not in left_out:
                            eng.wait_ge(pe_s.sem, pe_s.after("aff", t - 1))
                            tokens = slice((t - 1) * P, t * P) if isinstance(t, int) else bass.ds((t - 1) * P, P)
                            dve_s.done("aff", eng.tensor_scalar(aff_turned[:, tokens], bank[7][0:48, 0:P], 1.0, None, ALU.mult))
                        add(1, f"addb{s}")
                        if f"rmax{1 - s}" not in left_out:
                            eng.wait_ge(pe_s.sem, pe_s.after(f"r{1 - s}", before))
                            dve_s.done(f"rmax{1 - s}", eng.tensor_reduce(st[1 - s][:, 3:4], bank[6][:, 0:E], AX.X, ALU.max,
                                                                         negate=True))
                        if f"h{s}" not in left_out:
                            eng.wait_ge(pool_s.sem, pool_s.after(f"x{s}", t))
                            dve_s.done(f"h{s}", eng.scalar_tensor_tensor(
                                out=h[s], in0=xn[s], scalar=st[s][:, 2:3], in1=gain, op0=ALU.mult, op1=ALU.mult))
                        if f"recip{1 - s}" not in left_out:
                            eng.wait_ge(act_s.sem, act_s.after(f"exp{1 - s}", before))
                            dve_s.done(f"recip{1 - s}", eng.reciprocal(st[1 - s][:, 5:6], st[1 - s][:, 4:5]))
                            eng.wait_ge(dve_s.sem, dve_s.after(f"recip{1 - s}", before))
                            dve_s.done(f"aff{1 - s}", eng.tensor_scalar(
                                aff[:, 32 * (1 - s):32 * (1 - s) + E], logits[1 - s], st[1 - s][:, 5:6], None, ALU.mult))

                eng.memset(aff, 0.0).then_inc(aff_zero, 1)
                eng.wait_ge(aff_zero, 1)
                eng.wait_ge(const_in, 32)
                eng.wait_ge(pe_s.sem, pe_s.after("oT1 0", 0))
                take_rows(0).then_inc(dve_s.sem, 8)
                parts(eng, dve_s, body)

            def pool(eng):
                with eng.Fori(0, T) as t:
                    for s in range(2):
                        eng.wait_ge(act_s.sem, act_s.after(f"square{s}", t))
                        rsqrt_mean(eng, pool_s, f"x{s}", t, st[s][:, 0:1], st[s][:, 1:2], st[s][:, 2:3], D)

            end_stage(sp, pe, act, dve, pool)

        def choose(kind, layer):
            a = Arena()
            best = a.take(CAP, rows=48)
            where_u = a.take(CAP, rows=48).bitcast(U32)
            spread_i = a.take(P, rows=48)
            spread_v = a.take(P, rows=48)
            ROUNDS = CAP // 8
            zeroed = sem(f"{kind}_zeroed")
            names = []
            for r in range(ROUNDS):
                names += [f"max{r}", f"index{r}", f"replace{r}"]
            dve_s = Steps(counts, "dve", names + ["spread", "chosen"], 1)
            pe_s = Steps(counts, "pe", ["slots"], 1)

            def sp(eng):
                load_piece(eng, layer, 0, 4)
                load_piece(eng, layer, 0, 5)

            def act(eng):
                pass

            def pe(eng):
                eng.wait_ge(dve_s.sem, dve_s.after("spread"))
                eng.matmul(bank[0][:, 0:E], spread_i, rows_to_slots[:, :], start=True, stop=True)
                pe_s.done("slots", eng.matmul(bank[1][:, 0:E], spread_v, rows_to_slots[:, :], start=True, stop=True))

            def dve(eng):
                for r in range(ROUNDS):
                    c = slice(8 * r, 8 * r + 8)
                    if r:
                        eng.wait_ge(dve_s.sem, dve_s.after(f"replace{r - 1}"))
                    dve_s.done(f"max{r}", eng.max(best[:, c], aff_turned[:, :]))
                    eng.wait_ge(dve_s.sem, dve_s.after(f"max{r}"))
                    dve_s.done(f"index{r}", eng.max_index(where_u[:, c], best[:, c], aff_turned[:, :]))
                    dve_s.done(f"replace{r}", eng.match_replace(aff_turned[:, :], best[:, c], aff_turned[:, :], -1.0))
                eng.wait_ge(zeroed, 2)
                eng.wait_ge(dve_s.sem, dve_s.after(f"index{ROUNDS - 1}"))
                eng.tensor_copy(spread_i[0:16, 0:CAP], where_u[0:16, :])
                eng.tensor_scalar(spread_i[32:48, CAP:P], where_u[32:48, :], float(SEQ), None, ALU.add)
                eng.tensor_copy(spread_v[0:16, 0:CAP], best[0:16, :])
                dve_s.done("spread", eng.tensor_copy(spread_v[32:48, CAP:P], best[32:48, :]))
                eng.wait_ge(pe_s.sem, pe_s.after("slots"))
                eng.wait_ge(zeroed, 3)
                eng.tensor_copy(chosen[:, 0:E], bank[0][:, 0:E])
                dve_s.done("chosen", eng.tensor_copy(gates[:, 0:E], bank[1][:, 0:E]))

            def pool(eng):
                eng.memset(spread_i, 0.0).then_inc(zeroed, 1)
                eng.memset(spread_v, 0.0).then_inc(zeroed, 1)
                eng.memset(chosen[:, :].bitcast(F32), 0.0).then_inc(zeroed, 1)

            end_stage(sp, pe, act, dve, pool)

        SOURCES = [(w_gate, 0), (w_gate, 1), (w_up, 0), (w_up, 1), (w_down, 0), (w_down, 1)]

        def load_piece(eng, layer, e, k):
            w, half = SOURCES[k]
            eng.dma_start(ring[:, k * PIECE:(k + 1) * PIECE].rearrange("p (c n) -> p c n", c=4),
                          at(w, (e + layer * E) * (D * F) + half * (D * F // 2), [[F, P], [P * F, 4], [1, F]])
                          ).then_inc(piece_in[k], 16)

        def experts(layer, follow=None):
            a = Arena()
            rows = [a.take(D) for _ in range(2)]
            xT = [a.take(DC, P) for _ in range(2)]
            sig = a.take(F)
            gated = a.take(F)
            hidden = a.take(F)
            hT = a.take(DC, P)
            y = [a.take(D) for _ in range(2)]
            row_index = [a.take(1).bitcast(U32) for _ in range(2)]
            index = [a.take(1).bitcast(U32) for _ in range(2)]
            gate = [a.take(1) for _ in range(2)]
            piece = [ring[:, k * PIECE:(k + 1) * PIECE].rearrange("p (c n) -> p c n", c=4) for k in range(RING)]
            rows_in = [sem(f"rows_in{layer}{j}") for j in range(2)]
            scattered = sem(f"scattered{layer}")
            before = list(pieces)

            lags = {"h0": 1, "h1": 1, "down lo": 1, "down hi": 1, "hT": 1, "y": 1, "index": 1, "gate": 1,
                    "x0": -1, "x1": -1, "xT": -1, "row index": -1}
            pe_names = ["gate lo", "h0", "h1", "gate hi", "down lo", "down hi", "up lo", "x0", "x1", "up hi"]
            act_names = ["hT", "exp0", "exp1", "y", "xT"]
            dve_names = ["hT", "den0", "sig0", "silu0", "den1", "sig1", "silu1", "y", "xT", "hidden0", "hidden1"]
            pool_names = ["index", "gate", "row index"]
            pe_s = Steps(counts, "pe", pe_names, E + 1, lead=3, lags=lags)
            act_s = Steps(counts, "act", act_names, E + 1, lead=1, lags=lags)
            dve_s = Steps(counts, "dve", dve_names, E + 1, lead=3, lags=lags)
            pool_s = Steps(counts, "pool", pool_names, E + 1, lead=1, lags=lags)
            freed = ["gate lo", "gate hi", "up lo", "up hi", "down lo", "down hi"]

            def rounds(eng, steps, body):
                first = [m for m in steps.names if lags.get(m) == 1]
                tail = [m for m in steps.names if lags.get(m) != 1]
                steps.part(first)
                body(0, 0, first)
                steps.part()
                body(1, 1, ())
                with eng.Fori(1, E // 2) as pair:
                    for j in range(2):
                        body(pair * 2 + j, j, ())
                steps.part(tail)
                body(E, 0, tail)

            def sp(eng):
                def load(e, k, ahead):
                    eng.wait_ge(pe_s.sem, pe_s.after(freed[k], e + (ahead - 1)))
                    load_piece(eng, layer, e + ahead, k)

                for k in range(4):
                    load(0, k, 1)
                with eng.Fori(1, E - 1) as e:
                    for k in (0, 1):
                        load(e, k, 1)
                    for k in (4, 5):
                        load(e, k, 0)
                    for k in (2, 3):
                        load(e, k, 1)
                for k in (4, 5):
                    load(E - 1, k, 0)
                if follow:
                    for k in range(4):
                        eng.wait_ge(pe_s.sem, pe_s.after(freed[k], E - 1))
                        follow(eng, k)

            def turn(eng, src, k, done):
                for c in range(4):
                    mm = eng.transpose(bank[k][:, c * P:(c + 1) * P],
                                       src[:, (4 * k + c) * P:(4 * k + c + 1) * P], ident[:, :])
                done(mm)

            def pe(eng):
                def body(e, j, left_out):
                    def product(first_bank, lhs, k, half, name, n):
                        eng.wait_ge(piece_in[k], n * 16 + (16 * before[k] + 16))
                        for c in range(4):
                            for b in range(2):
                                mm = eng.matmul(bank[first_bank + b][:, :], lhs[:, 4 * half + c, :],
                                                piece[k][:, c, b * BANK:(b + 1) * BANK],
                                                start=(half == 0 and c == 0), stop=(half == 1 and c == 3))
                        pe_s.done(name, mm)

                    eng.wait_ge(act_s.sem, act_s.after("xT", e))
                    eng.wait_ge(dve_s.sem, dve_s.after("xT", e))
                    if "gate lo" not in left_out:
                        product(2, xT[j], 0, 0, "gate lo", e)
                    if "h0" not in left_out:
                        for k in range(2):
                            eng.wait_ge(dve_s.sem, dve_s.after(f"hidden{k}", e - 1))
                            turn(eng, hidden, k, lambda mm: pe_s.done(f"h{k}", mm))
                    if "gate hi" not in left_out:
                        product(2, xT[j], 1, 1, "gate hi", e)
                    if "down lo" not in left_out:
                        eng.wait_ge(act_s.sem, act_s.after("hT", e - 1))
                        eng.wait_ge(dve_s.sem, dve_s.after("hT", e - 1))
                        product(6, hT, 4, 0, "down lo", e - 1)
                        product(6, hT, 5, 1, "down hi", e - 1)
                    if "up lo" not in left_out:
                        product(4, xT[j], 2, 0, "up lo", e)
                        eng.wait_ge(rows_in[1 - j], e * 8 + (24 if j else 16))
                        for k in range(2):
                            turn(eng, rows[1 - j], k, lambda mm: pe_s.done(f"x{k}", mm))
                        product(4, xT[j], 3, 1, "up hi", e)

                eng.wait_ge(rows_in[0], 16)
                turn(eng, rows[0], 0, lambda mm: mm.then_inc(pe_s.sem, 1))
                turn(eng, rows[0], 1, lambda mm: mm.then_inc(pe_s.sem, 2))
                rounds(eng, pe_s, body)

            def act(eng):
                def take(out, k):
                    return eng.activation(out.rearrange("p a b -> p (a b)")[:, 0:512], bank[k][:, :], ACT.Copy)

                def body(e, j, left_out):
                    if "hT" not in left_out:
                        eng.wait_ge(pe_s.sem, pe_s.after("h0", e - 1))
                        act_s.done("hT", take(hT, 0))
                    if "exp0" not in left_out:
                        eng.wait_ge(pe_s.sem, pe_s.after("gate hi", e))
                        for k in range(2):
                            eng.wait_ge(dve_s.sem, dve_s.after(f"silu{k}", e - 1))
                            act_s.done(f"exp{k}", eng.activation(sig[:, k * 512:(k + 1) * 512], bank[2 + k][:, :],
                                                                 ACT.Exp, scale=-1.0))
                    if "y" not in left_out:
                        eng.wait_ge(pe_s.sem, pe_s.after("down hi", e - 1))
                        eng.wait_ge(pool_s.sem, pool_s.after("gate", e - 1))
                        act_s.done("y", eng.activation(y[1 - j][:, 0:512], bank[6][:, :], ACT.Copy, scale=gate[1 - j]))
                    if "xT" not in left_out:
                        eng.wait_ge(pe_s.sem, pe_s.after("x0", e + 1))
                        act_s.done("xT", take(xT[1 - j], 0))

                eng.wait_ge(pe_s.sem, pe_s.after("x0", 0))
                take(xT[0], 0).then_inc(act_s.sem, 2)
                act_s.skip(1)
                rounds(eng, act_s, body)

            def dve(eng):
                def take(out, k):
                    return eng.tensor_copy(out.rearrange("p a b -> p (a b)")[:, 512:1024], bank[k][:, :])

                def body(e, j, left_out):
                    if "hT" not in left_out:
                        eng.wait_ge(pe_s.sem, pe_s.after("h1", e - 1))
                        dve_s.done("hT", take(hT, 1))
                    if "den0" not in left_out:
                        for k in range(2):
                            half = slice(k * 512, (k + 1) * 512)
                            eng.wait_ge(act_s.sem, act_s.after(f"exp{k}", e))
                            dve_s.done(f"den{k}", eng.tensor_scalar(sig[:, half], sig[:, half], 1.0, None, ALU.add))
                            eng.wait_ge(dve_s.sem, dve_s.after(f"den{k}", e))
                            dve_s.done(f"sig{k}", eng.reciprocal(sig[:, half], sig[:, half]))
                            eng.wait_ge(dve_s.sem, dve_s.after(f"sig{k}", e))
                            dve_s.done(f"silu{k}", eng.tensor_tensor(gated[:, half], bank[2 + k][:, :], sig[:, half], ALU.mult))
                    if "y" not in left_out:
                        eng.wait_ge(pe_s.sem, pe_s.after("down hi", e - 1))
                        eng.wait_ge(pool_s.sem, pool_s.after("gate", e - 1))
                        dve_s.done("y", eng.tensor_scalar(y[1 - j][:, 512:1024], bank[7][:, :], gate[1 - j], None, ALU.mult))
                    if "xT" not in left_out:
                        eng.wait_ge(pe_s.sem, pe_s.after("x1", e + 1))
                        dve_s.done("xT", take(xT[1 - j], 1))
                        eng.wait_ge(pe_s.sem, pe_s.after("up hi", e))
                        for k in range(2):
                            half = slice(k * 512, (k + 1) * 512)
                            eng.wait_ge(dve_s.sem, dve_s.after(f"silu{k}", e))
                            dve_s.done(f"hidden{k}", eng.tensor_tensor(hidden[:, half], bank[4 + k][:, :], gated[:, half], ALU.mult))

                eng.wait_ge(pe_s.sem, pe_s.after("x1", 0))
                take(xT[0], 1).then_inc(dve_s.sem, 4)
                dve_s.skip(1)
                rounds(eng, dve_s, body)

            def pool(eng):
                def column(m, e):
                    return m[:, e:e + 1] if isinstance(e, int) else m[:, bass.ds(e, 1)]

                def gather(e, j, n, steps=None):
                    eng.wait_ge(pe_s.sem, pe_s.after("x1", n - 2))
                    passed(eng)
                    copy = eng.tensor_copy(row_index[j], column(chosen, e))
                    if steps:
                        pool_s.done("row index", copy)
                    else:
                        copy.then_inc(pool_s.sem, 3)
                        pool_s.skip(2)
                    eng.wait_ge(pool_s.sem, pool_s.after("row index", n))
                    passed(eng)
                    eng.indirect_dma_start(out=rows[j], out_offset=None, in_=normed,
                                           in_offset=bass.IndirectOffsetOnAxis(ap=row_index[j], axis=0)).then_inc(rows_in[j], 16)

                def body(e, j, left_out):
                    if "index" not in left_out:
                        if not isinstance(e, int) or e > 1:
                            eng.wait_ge(scattered, (e - 1) * 16)
                        passed(eng)
                        pool_s.done("index", eng.tensor_copy(index[1 - j], column(chosen, e - 1)))
                        pool_s.done("gate", eng.tensor_copy(gate[1 - j], column(gates, e - 1)))
                    if "row index" not in left_out:
                        gather(e + 1, 1 - j, e + 1, True)
                    if "index" not in left_out:
                        eng.wait_ge(pool_s.sem, pool_s.after("index", e - 1))
                        eng.wait_ge(act_s.sem, act_s.after("y", e - 1))
                        eng.wait_ge(dve_s.sem, dve_s.after("y", e - 1))
                        passed(eng)
                        eng.indirect_dma_start(out=residual, out_offset=bass.IndirectOffsetOnAxis(ap=index[1 - j], axis=0),
                                               in_=y[1 - j], in_offset=None, compute_op=ALU.add).then_inc(scattered, 16)

                gather(0, 0, 0)
                rounds(eng, pool_s, body)
                eng.wait_ge(scattered, 16 * E)
                eng.wait_ge(rows_in[0], 16 * (E // 2 + 1))

            for k in range(RING):
                pieces[k] += E
            end_stage(sp, pe, act, dve, pool)

        def finish():
            a = Arena()
            gain = a.take(D)
            ROUNDS = SEQS * T
            xt = a.take(ROUNDS, D)
            yt = a.take(ROUNDS, D)
            total, mean, scale = a.take(ROUNDS), a.take(ROUNDS), a.take(ROUNDS)
            gain_in = sem("final_gain_in")
            rows_in = [sem(f"final_rows_in{n}") for n in range(ROUNDS)]
            y_stored = sem("y_stored")
            act_s = Steps(counts, "act", ["square"], ROUNDS)
            pool_s = Steps(counts, "pool", ["x mean", "x eps", "x"], ROUNDS)
            dve_s = Steps(counts, "dve", ["y"], ROUNDS)

            def sp(eng):
                tile = [[D, P], [1, D]]
                for n in range(ROUNDS):
                    eng.dma_start(xt[:, n, :], at(residual, n * P * D, tile)).then_inc(rows_in[n], 16)
                    if n == 0:
                        eng.dma_start(gain, at(norm_final, 0, [[0, P], [1, D]])).then_inc(gain_in, 16)
                for n in range(ROUNDS):
                    eng.wait_ge(dve_s.sem, dve_s.after("y", n))
                    eng.dma_start(at(y_out, n * P * D, tile), yt[:, n, :]).then_inc(y_stored, 16)
                eng.wait_ge(y_stored, 16 * ROUNDS)

            def pe(eng):
                pass

            def act(eng):
                for n in range(ROUNDS):
                    eng.wait_ge(rows_in[n], 16)
                    act_s.done("square", eng.activation(yt[:, n, :], xt[:, n, :], ACT.Square, accum_out=total[:, n:n + 1]))

            def pool(eng):
                for n in range(ROUNDS):
                    eng.wait_ge(act_s.sem, act_s.after("square", n))
                    k = slice(n, n + 1)
                    rsqrt_mean(eng, pool_s, "x", n, total[:, k], mean[:, k], scale[:, k], D)

            def dve(eng):
                eng.wait_ge(gain_in, 16)
                for n in range(ROUNDS):
                    eng.wait_ge(pool_s.sem, pool_s.after("x", n))
                    dve_s.done("y", eng.scalar_tensor_tensor(out=yt[:, n, :], in0=xt[:, n, :], scalar=scale[:, n:n + 1],
                                                             in1=gain, op0=ALU.mult, op1=ALU.mult))

            end_stage(sp, pe, act, dve, pool)

        def first_of(inputs):
            def load(eng):
                for s in range(2):
                    inputs.load_first(eng, s)
            return load

        mla = AttentionInputs("mla", 4 * PIECE, ring, 6 * PIECE)
        window = AttentionInputs("window", 7168)
        dilated = AttentionInputs("dilated", 20480)
        grid = AttentionInputs("grid", 8192)
        output_ab = OutputInputs("ab", 0, x_in)
        output_cd = OutputInputs("cd", 1, residual)

        plan = [start,
                lambda: project("ab", 0, x_in, mla),
                lambda: attention(mla, 0, 0, prefetch=lambda eng: spread_biases(eng, (0, 1)), zero_next=window.zero, next_early=first_of(window)),
                lambda: attention(window, H * MV, 7168 + 6144, prefetch=load_w_out("ab", w_out_ab),
                                  next_early=output_ab.load_early, next_late=lambda eng: output_ab.load_rows(eng, 0)),
                lambda: output(output_ab),
                lambda: choose("ab", 0),
                lambda: experts(0, follow=load_cd_weights),
                lambda: project("cd", 1, residual, dilated),
                lambda: attention(dilated, 0, 0, prefetch=load_w_out("cd", w_out_cd), zero_next=grid.zero,
                                  next_early=first_of(grid)),
                lambda: attention(grid, H * HD, 8192 + 7168,
                                  next_early=output_cd.load_early, next_late=lambda eng: output_cd.load_rows(eng, 0)),
                lambda: output(output_cd),
                lambda: choose("cd", 1),
                lambda: experts(1),
                finish]
        for stage in plan:
            stage()

        with nc.Block() as block:
            @block.sync
            def _(eng):
                for program in block_programs["sp"]:
                    program(eng)

            @block.tensor
            def _(eng):
                for program in block_programs["pe"]:
                    program(eng)

            @block.scalar
            def _(eng):
                for program in block_programs["act"]:
                    program(eng)

            @block.vector
            def _(eng):
                for program in block_programs["dve"]:
                    program(eng)

            @block.gpsimd
            def _(eng):
                for program in block_programs["pool"]:
                    program(eng)


def rope_rows():
    import numpy as np

    def angles(dim):
        inv = (1.0 / (np.float32(10000.0) ** (np.arange(0, dim, 2, dtype=np.float32) / dim))).astype(np.float32)
        a = (np.arange(SEQ, dtype=np.float32)[:, None] * inv[None, :]).astype(np.float64)
        return np.cos(a).astype(np.float32), np.sin(a).astype(np.float32)
    c, s = angles(HD)
    cos, sin = np.concatenate([c, c], 1), np.concatenate([-s, s], 1)
    scale = np.float32(HD ** -0.5)
    c, s = angles(ROPE)
    small = np.concatenate([c, c, -s, s], 1)
    return np.ascontiguousarray(np.concatenate([cos * scale, sin * scale, cos, sin, small, small], 1).astype(np.float32))


def key_tables():
    import numpy as np
    d = np.arange(SPAN)[None, :] - (SEQ - P) - np.arange(P)[:, None]
    window = np.where(np.abs(d) <= 128, 0.0, NEG).astype(np.float32)
    times = (np.abs(d) <= 64).astype(int) + ((d % 4 == 0) & (np.abs(d) <= 256)) + (d % 16 == 0)
    dilated = np.where(times > 0, np.log(np.maximum(times, 1)), NEG).astype(np.float32)
    c = np.arange(P)[:, None] % GRID_W
    first = np.clip(c - 8, 0, GRID_W - 16)
    k = np.arange(GRID_W)[None, :]
    columns = np.where((k >= first) & (k < first + 16), 0.0, NEG).astype(np.float32)
    return window, dilated, columns


def host_arrays(inputs):
    import numpy as np
    g = {n: np.asarray(a) for n, a in inputs.items()}
    window, dilated, columns = key_tables()
    return {
        "x_in": np.concatenate([g["x_prompt"][0], g["x_sample"][0]], 0),
        "norm_mix": g["norm_mix"], "norm_ffn": g["norm_ffn"], "norm_final": g["norm_final"],
        "w_in_ab": g["w_in_ab"][0], "q_norm": g["mla_q_norm"], "w_uq": g["mla_w_uq"][0],
        "kv_norm": g["mla_kv_norm"], "w_ukv": g["mla_w_ukv"][0], "sink": g["swa_sink"],
        "w_out_ab": g["w_out_ab"][0], "w_in_cd": g["w_in_cd"][0],
        "rpb_padded": np.pad(g["na_rpb"][0], ((0, 0), (0, 0), (48, P - 48 - 31))),
        "w_out_cd": g["w_out_cd"][0], "w_router": g["w_router"], "w_gate": g["w_gate"],
        "w_up": g["w_up"], "w_down": g["w_down"],
        "rope_table": rope_rows(), "window_table": window, "dilated_table": dilated, "column_table": columns,
    }


def kernel(**inputs):
    import numpy as _np
    import concourse.bacc as _bacc
    from concourse import mybir as _mybir
    from concourse.bass_utils import run_bass_kernel_spmd as _run

    nc = _bacc.Bacc("TRN2", target_bir_lowering=False, num_devices=1)
    arrays, args = {}, {}
    for name, a in host_arrays(inputs).items():
        a = _np.ascontiguousarray(a)
        arrays[f"in_{name}"] = a
        args[name] = nc.dram_tensor(f"in_{name}", a.shape, _mybir.dt.from_np(a.dtype), kind="ExternalInput").ap()
    args["y_out"] = nc.dram_tensor("y_out", (TOK, D), _mybir.dt.float32, kind="ExternalOutput").ap()
    hybrid_trunk(nc, **args)
    r = _run(nc, [arrays], core_ids=[0])
    y = r.results[0]["y_out"]
    return y[None, 0:SEQ], y[None, SEQ:TOK]
```
